# Optimizing a Trainium2 kernel written in Bass

```python
import jax, jax.numpy as jnp
from jax import lax
import numpy as np

D_MODEL = 1024
BATCH = 1
SEQ = 256
DEPTH = 2

MEM_LEN = 256
N_XA_HEADS = 4
XA_HEAD_DIM = D_MODEL // N_XA_HEADS
POOL_WINDOWS = (2, 4, 8, 16)
N_POOL_GROUPS = len(POOL_WINDOWS)
POOL_GROUP_DIM = D_MODEL // N_POOL_GROUPS
CONV_WIDTH = 31
D_FF = (D_MODEL * 7) // 2
N_EXPERTS = 8
TOP_K = 2
N_MIXERS = 2
N_EVEN = (DEPTH + 1) // 2
N_ODD = DEPTH // 2
EPS = 1e-6

kernel_name = "hybrid_pool_conformer_memxattn_moe"

def rms_norm(x, g):
    xf = x.astype(jnp.float32)
    y = xf * lax.rsqrt(jnp.mean(xf * xf, axis=-1, keepdims=True) + EPS)
    return (y * g.astype(jnp.float32)).astype(x.dtype)

def layer_norm(x, g, b):
    xf = x.astype(jnp.float32)
    mu = jnp.mean(xf, axis=-1, keepdims=True)
    xc = xf - mu
    var = jnp.mean(xc * xc, axis=-1, keepdims=True)
    y = xc * lax.rsqrt(var + EPS)
    return (y * g.astype(jnp.float32) + b.astype(jnp.float32)).astype(x.dtype)

def pool_mixer(h, w_grp, b_grp, scale):
    B, S, D = h.shape
    hf = h.astype(jnp.float32)
    csum = jnp.cumsum(hf, axis=1).reshape(B, S, N_POOL_GROUPS, POOL_GROUP_DIM)
    pos = jnp.arange(S)
    pooled = []
    for g, w in enumerate(POOL_WINDOWS):
        c = csum[:, :, g]
        c_prev = jnp.pad(c, ((0, 0), (w, 0), (0, 0)))[:, :S]
        cnt = jnp.minimum(pos + 1, w).astype(jnp.float32)[None, :, None]
        pooled.append((c - c_prev) / cnt)
    pooled = jnp.stack(pooled, axis=2) - hf.reshape(B, S, N_POOL_GROUPS, POOL_GROUP_DIM)
    y = jnp.einsum("bsgc,gcd->bsgd", pooled.astype(h.dtype), w_grp) + b_grp
    return y.reshape(B, S, D) * scale

def conv_module(h, pw1_w, pw1_b, dw_w, dw_b, ln_g, ln_b, pw2_w, pw2_b):
    D = h.shape[-1]
    a = h @ pw1_w + pw1_b
    u = a[..., :D] * jax.nn.sigmoid(a[..., D:])
    u_pad = jnp.pad(u, ((0, 0), (CONV_WIDTH - 1, 0), (0, 0)))
    v = lax.conv_general_dilated(
        u_pad, dw_w[:, None, :], window_strides=(1,), padding="VALID",
        dimension_numbers=("NWC", "WIO", "NWC"), feature_group_count=D) + dw_b
    v = jax.nn.silu(layer_norm(v, ln_g, ln_b))
    return v @ pw2_w + pw2_b

def mem_cross_attention(h, mem_n, wq, wkv, wo):
    B, S, D = h.shape
    M = mem_n.shape[1]
    q = (h @ wq).reshape(B, S, N_XA_HEADS, XA_HEAD_DIM)
    kv = mem_n @ wkv
    k = kv[..., :D].reshape(B, M, N_XA_HEADS, XA_HEAD_DIM)
    v = kv[..., D:].reshape(B, M, N_XA_HEADS, XA_HEAD_DIM)
    scores = jnp.einsum("bshd,bmhd->bhsm", q, k).astype(jnp.float32) * (XA_HEAD_DIM ** -0.5)
    p = jax.nn.softmax(scores, axis=-1).astype(v.dtype)
    o = jnp.einsum("bhsm,bmhd->bshd", p, v).reshape(B, S, D)
    return o @ wo

def swiglu(h, w_gu, w_down):
    gu = h @ w_gu
    return (jax.nn.silu(gu[..., :D_FF]) * gu[..., D_FF:]) @ w_down

def moe_swiglu(h, w_router, w_gu, w_down):
    logits = (h @ w_router).astype(jnp.float32)
    top_vals, top_idx = lax.top_k(logits, TOP_K)
    top_w = jax.nn.softmax(top_vals, axis=-1)
    gates = jnp.sum(jax.nn.one_hot(top_idx, N_EXPERTS, dtype=jnp.float32) * top_w[..., None], axis=-2)
    out = jnp.zeros_like(h)
    for e in range(N_EXPERTS):
        out = out + swiglu(h, w_gu[e], w_down[e]) * gates[..., e:e + 1].astype(h.dtype)
    return out

def setup_inputs(seed: int = 0) -> dict:
    key = jax.random.key(seed)
    ks = iter(jax.random.split(key, 32))
    D, F, E = D_MODEL, D_FF, N_EXPERTS

    def nrm(shape, scale):
        return jax.random.normal(next(ks), shape, jnp.float32) * scale

    def gain(shape):
        return 1.0 + nrm(shape, 0.05)

    return {
        "x": nrm((BATCH, SEQ, D), 1.0),
        "mem": nrm((BATCH, MEM_LEN, D), 1.0),
        "mem_norm_g": gain((D,)),
        "mix_pre_g": gain((DEPTH, D)),
        "mix_post_g": gain((DEPTH, D)),
        "xa_pre_g": gain((DEPTH, D)),
        "xa_post_g": gain((DEPTH, D)),
        "ffn_pre_g": gain((DEPTH, D)),
        "ffn_post_g": gain((DEPTH, D)),
        "xa_wq": nrm((DEPTH, D, D), D ** -0.5),
        "xa_wkv": nrm((DEPTH, D, 2 * D), D ** -0.5),
        "xa_wo": nrm((DEPTH, D, D), D ** -0.5),
        "pool_w": nrm((N_EVEN, N_POOL_GROUPS, POOL_GROUP_DIM, POOL_GROUP_DIM), POOL_GROUP_DIM ** -0.5),
        "pool_b": nrm((N_EVEN, N_POOL_GROUPS, POOL_GROUP_DIM), 0.02),
        "pool_scale": 1.0 + nrm((N_EVEN, D), 0.1),
        "conv_pw1_w": nrm((N_ODD, D, 2 * D), D ** -0.5),
        "conv_pw1_b": nrm((N_ODD, 2 * D), 0.02),
        "conv_dw_w": nrm((N_ODD, CONV_WIDTH, D), CONV_WIDTH ** -0.5),
        "conv_dw_b": nrm((N_ODD, D), 0.02),
        "conv_ln_g": gain((N_ODD, D)),
        "conv_ln_b": nrm((N_ODD, D), 0.02),
        "conv_pw2_w": nrm((N_ODD, D, D), D ** -0.5),
        "conv_pw2_b": nrm((N_ODD, D), 0.02),
        "ffn_w_gu": nrm((N_EVEN, D, 2 * F), D ** -0.5),
        "ffn_w_down": nrm((N_EVEN, F, D), F ** -0.5),
        "moe_router": nrm((N_ODD, D, E), D ** -0.5),
        "moe_w_gu": nrm((N_ODD, E, D, 2 * F), D ** -0.5),
        "moe_w_down": nrm((N_ODD, E, F, D), F ** -0.5),
    }

def reference(x, mem, mem_norm_g, mix_pre_g, mix_post_g, xa_pre_g, xa_post_g,
              ffn_pre_g, ffn_post_g, xa_wq, xa_wkv, xa_wo, pool_w, pool_b,
              pool_scale, conv_pw1_w, conv_pw1_b, conv_dw_w, conv_dw_b,
              conv_ln_g, conv_ln_b, conv_pw2_w, conv_pw2_b, ffn_w_gu,
              ffn_w_down, moe_router, moe_w_gu, moe_w_down):
    mem_n = rms_norm(mem, mem_norm_g)
    for i in range(DEPTH):
        j = i // 2
        hn = rms_norm(x, mix_pre_g[i])
        if i % N_MIXERS == 0:
            y = pool_mixer(hn, pool_w[j], pool_b[j], pool_scale[j])
        else:
            y = conv_module(hn, conv_pw1_w[j], conv_pw1_b[j], conv_dw_w[j], conv_dw_b[j],
                            conv_ln_g[j], conv_ln_b[j], conv_pw2_w[j], conv_pw2_b[j])
        x = x + rms_norm(y, mix_post_g[i])
        y = mem_cross_attention(rms_norm(x, xa_pre_g[i]), mem_n, xa_wq[i], xa_wkv[i], xa_wo[i])
        x = x + rms_norm(y, xa_post_g[i])
        hn = rms_norm(x, ffn_pre_g[i])
        if i % 2 == 0:
            y = swiglu(hn, ffn_w_gu[j], ffn_w_down[j])
        else:
            y = moe_swiglu(hn, moe_router[j], moe_w_gu[j], moe_w_down[j])
        x = x + rms_norm(y, ffn_post_g[i])
    return x


_drawn_inputs = setup_inputs


def setup_inputs(seed=0):
    import zlib

    import numpy as np

    out = dict(_drawn_inputs(seed))
    spreads = {}
    factors = {}
    for name, (base, spread) in spreads.items():
        noise = np.random.default_rng([zlib.crc32(name.encode()), seed]).standard_normal(out[name].shape)
        drawn = base * np.exp(spread * noise) if base else spread * noise
        out[name] = __import__('jax').numpy.asarray(drawn.astype(out[name].dtype))
    for name, factor in factors.items():
        out[name] = (out[name] * factor).astype(out[name].dtype)
    return out
```

```python
from contextlib import ExitStack

import numpy as np

import concourse.bass as bass
from concourse import mybir

F32 = mybir.dt.float32
F32R = mybir.dt.float32r
I32 = mybir.dt.int32
ALU = mybir.AluOpType
ACT = mybir.ActivationFunctionType
AX = mybir.AxisListType

P = 128
D = 1024
S = 256
F = 3584
E = 8
HEADS = 4
TAPS = 31
WINDOWS = (2, 4, 8, 16)
EPS = 1e-6
NB = S // P
NC = D // P
UNIT = 2048
RING = 6
SPLIT = 3
SHARE = 1792
NT = 512
STEPS = F // NT
PER_STEP = 6
PER_FFN = STEPS * PER_STEP
SLOTS = 128
PAD = 16
CPAD = TAPS - 1
BIG = 3.0e38
SCALE = float(D // HEADS) ** -0.5
COMBINE_BANKS = (5, 6, 0, 1)

_at = 0
U = {}
for _name, _n in (("k0", 4), ("v0", 4), ("pool", 1), ("q0", 4), ("o0", 4), ("ffn", PER_FFN), ("pw1", 8), ("k1", 4),
                  ("v1", 4), ("pw2", 4), ("q1", 4), ("o1", 4), ("moe", E * PER_FFN)):
    U[_name] = _at
    _at += _n
UNITS = _at

COL = {}
_at = 0
for _name, _n in (("mem", NC), ("mix0", NC), ("xa0", NC), ("ffn0", NC), ("mix1", NC), ("xa1", NC), ("ffn1", NC),
                  ("pw1_b", 2 * NC), ("dw_b", NC), ("ln_g", NC), ("ln_b", NC), ("dw_w", TAPS * NC), ("router", NC * E)):
    COL[_name] = _at
    _at += _n
COLS = _at
ROWS = ("recip", "pool_b", "pool_scale", "mix_post0", "xa_post0", "ffn_post0", "pw2_b", "mix_post1", "xa_post1", "ffn_post1")
ROW_SLOTS = 3

STAT = {n: i for i, n in enumerate(("mem", "mix0", "post_mix0", "xa0", "post_xa0", "ffn0", "post_ffn0", "mix1",
                                    "post_mix1", "xa1", "post_xa1", "ffn1", "post_ffn1"))}
TURN = {n: i for i, n in enumerate(("mem", "mix0", "xa0", "ffn0", "mix1", "mem_again", "xa1", "ffn1"))}
XT = {n: i for i, n in enumerate(("mem", "pooled", "xa0", "o0", "ffn0", "mix1", "mem_again", "z", "xa1", "o1", "gather"))}
RES = {n: i for i, n in enumerate(("mix0", "xa0", "ffn0", "mix1", "xa1"))}
POST = {n: i for i, n in enumerate(("post_mix0", "post_xa0", "post_ffn0", "post_mix1", "post_xa1", "post_ffn1"))}


def unit(n):
    return n // RING, n % RING


def plus(u, k):
    return u[0] + (u[1] + k) // RING, (u[1] + k) % RING


def build(nc, x, mem, stream, cols, rows, out):
    with ExitStack() as ctx:
        def sb(name, shape, dt=F32):
            return ctx.enter_context(nc.sbuf_tensor(name, shape, dt))

        def sem(name):
            return ctx.enter_context(nc.semaphore(name))

        raw = sb("raw", [P, RING, UNIT])
        w_hi = sb("w_hi", [P, SPLIT, UNIT], F32R)
        w_lo = sb("w_lo", [P, SPLIT, UNIT], F32R)
        xt_hi = sb("xt_hi", [P, NC * S], F32R)
        xt_lo = sb("xt_lo", [P, NC * S], F32R)
        hn_hi = sb("hn_hi", [P, 2 * D], F32R)
        hn_lo = sb("hn_lo", [P, 2 * D], F32R)
        ys_hi = sb("ys_hi", [P, D], F32R)
        ys_lo = sb("ys_lo", [P, D], F32R)
        res = sb("res", [P, NB, D])
        buf_k = sb("buf_k", [P, NC, S])
        buf_v = sb("buf_v", [P, NB, D])
        buf_a = sb("buf_a", [P, NC * (S + CPAD)])
        buf_b = sb("buf_b", [P, NC * (S + PAD)])
        buf_c = sb("buf_c", [P, NC * (S + PAD)])
        row = sb("row", [P, ROW_SLOTS, D])
        col = sb("col", [P, COLS])
        ident = sb("ident", [P, P])
        ones = sb("ones", [P, P])
        upper = sb("upper", [P, P])
        iota = sb("iota", [P, SLOTS])
        rank = sb("rank", [P, E])
        zeros = sb("zeros", [P, P], F32R)
        eps = sb("eps", [P, 1])
        silu_at = sb("silu_at", [P, 1])
        stat = sb("stat", [P, 3, len(STAT), NB])
        soft = sb("soft", [P, 4, HEADS * NB])
        ln_row = sb("ln_row", [P, 2, S])
        sel = sb("sel", [P, SLOTS * NB], F32R)
        sel_t = sb("sel_t", [P, SLOTS * NB], F32R)
        route = sb("route", [P, 10, NB, E])
        rtmp = sb("rtmp", [P, 8, NB])
        place = sb("place", [P, E + 1, NB])
        place2 = sb("place2", [P, E + 1, NB])
        gate = sb("gate", [P, E + 1, NB])
        slot_gate = sb("slot_gate", [P, 1])
        over = sb("over", [P, 1])
        over_i = sb("over_i", [P, 1], I32)
        ps = ctx.enter_context(nc.psum_tensor("ps", [P, 8, NT], F32))

        landed = [sem(f"landed{i}") for i in range(RING)]
        s_hi = sem("s_hi")
        s_lo_v = sem("s_lo_v")
        s_lo_p = sem("s_lo_p")
        s_used = sem("s_used")
        s_in, s_col, s_mem, s_mem2 = sem("s_in"), sem("s_col"), sem("s_mem"), sem("s_mem2")
        s_row = [sem(f"s_row{i}") for i in range(ROW_SLOTS)]
        s_const, s_zero, s_init = sem("s_const"), sem("s_zero"), sem("s_init")
        s_sq = sem("s_sq")
        s_xn, s_turn = sem("s_xn"), sem("s_turn")
        s_xth, s_xtl = sem("s_xth"), sem("s_xtl")
        s_res, s_t = sem("s_res"), sem("s_t")
        s_f0, s_pad, s_win, s_pd, s_pb = (sem(n) for n in ("s_f0", "s_pad", "s_win", "s_pd", "s_pb"))
        s_kc, s_vc, s_qc = (sem(n) for n in ("s_kc", "s_vc", "s_qc"))
        s_sc, s_nm, s_ex, s_pn = (sem(n) for n in ("s_sc", "s_nm", "s_ex", "s_pn"))
        s_pt, s_pte, s_pto, s_ov = (sem(n) for n in ("s_pt", "s_pte", "s_pto", "s_ov"))
        s_silu, s_mul, s_ht, s_hth, s_htl = (sem(n) for n in ("s_silu", "s_mul", "s_ht", "s_hth", "s_htl"))
        m_silu, m_mul, m_ht, m_hth, m_htl = (sem(n) for n in ("m_silu", "m_mul", "m_ht", "m_hth", "m_htl"))
        m_steps = (m_silu, m_mul, m_ht, m_hth, m_htl)
        s_sg, s_u, s_cv, s_ln, s_mu, s_xc, s_vq, s_vs, s_lr, s_ly, s_z, s_p2 = (
            sem(n) for n in ("s_sg", "s_u", "s_cv", "s_ln", "s_mu", "s_xc", "s_vq", "s_vs", "s_lr", "s_ly", "s_z", "s_p2"))
        s_hnh, s_hnl, s_rf, s_lg, s_rt, s_e2, s_e2x, s_sel, s_pos, s_over = (
            sem(n) for n in ("s_hnh", "s_hnl", "s_rf", "s_lg", "s_rt", "s_e2", "s_e2x", "s_sel", "s_pos", "s_over"))
        s_g, s_gath, s_gtp, s_gt, s_gs, s_ysh, s_ysl, s_comb, s_acc = (
            sem(n) for n in ("s_g", "s_gath", "s_gtp", "s_gt", "s_gs", "s_ysh", "s_ysl", "s_comb", "s_acc"))
        s_tab = sem("s_tab")
        s_fin0, s_fin, s_out = sem("s_fin0"), sem("s_fin"), sem("s_out")

        block = ctx.enter_context(nc.Block())

        xth = xt_hi[:, :].rearrange("p (c t) -> p c t", c=NC)
        xtl = xt_lo[:, :].rearrange("p (c t) -> p c t", c=NC)
        tok_a = buf_a[:, 0:NB * D].rearrange("p (b d) -> p b d", b=NB)
        tok_b = buf_b[:, 0:NB * D].rearrange("p (b d) -> p b d", b=NB)
        tok_c = buf_c[:, 0:NB * D].rearrange("p (b d) -> p b d", b=NB)
        chan_a = buf_a[:, 0:NC * S].rearrange("p (c t) -> p c t", c=NC)
        chan_b = buf_b[:, 0:NC * S].rearrange("p (c t) -> p c t", c=NC)
        chan_c = buf_c[:, 0:NC * S].rearrange("p (c t) -> p c t", c=NC)
        pool_a, pool_b, pool_c = (b[:, 0:NC * (S + PAD)].rearrange("p (c t) -> p c t", c=NC) for b in (buf_a, buf_b, buf_c))
        conv_u = buf_a[:, :].rearrange("p (c t) -> p c t", c=NC)
        acc = buf_k[:, :, :].rearrange("p (b c) t -> p b (c t)", b=NB)
        sg_glu = buf_v[:, 0, 0:2 * S].rearrange("p (i t) -> p i t", i=2)
        y_ps = ps[:, 0:4, :].rearrange("p (b n) c -> p b n c", b=NB)
        y_tok = ps[:, 0:4, :].rearrange("p (b n) c -> p b (n c)", b=NB)

        def pooled(c):
            return (pool_b, pool_c)[c // 2 % 2][:, c, PAD:PAD + S]

        def gain(name, c):
            return col[:, COL[name] + c:COL[name] + c + 1]

        def turned(bank0, c):
            return ps[:, bank0 + c // 2, (c % 2) * S:(c % 2) * S + S]

        def wait_used(eng, u, lag):
            q, r = u
            if isinstance(q, int) and RING * q + r - lag + 1 <= 0:
                return
            eng.wait_ge(s_used, RING * q + (r - lag + 1))

        def wait_step(eng, s, count):
            if s in m_steps:
                eng.wait_ge(s, count + 1)
            elif not (isinstance(count, int) and count == 0):
                eng.wait_ge(s, count)

        def wait_low(eng, u):
            q, r = u
            eng.wait_ge(s_lo_v, RING * q + (r + 1))
            eng.wait_ge(s_lo_p, RING * q + (r + 1))

        def split_hi(act, u):
            q, r = u
            act.wait_ge(landed[r], 16 * (q + 1))
            wait_used(act, u, SPLIT)
            nc.scalar.activation(w_hi[:, r % SPLIT, :], raw[:, r, :], ACT.Copy).then_inc(s_hi, 1)

        def split_lo(dve, u):
            q, r = u
            dve.wait_ge(s_hi, RING * q + (r + 1))
            nc.vector.tensor_tensor(w_lo[:, r % SPLIT, 0:SHARE], raw[:, r, 0:SHARE], w_hi[:, r % SPLIT, 0:SHARE].bitcast(F32),
                                    ALU.subtract).then_inc(s_lo_v, 1)

        def load(sp, u, index):
            q, r = u
            if not (isinstance(q, int) and q == 0):
                sp.wait_ge(s_lo_v, RING * q + (r + 1 - RING))
                sp.wait_ge(s_lo_p, RING * q + (r + 1 - RING))
            sp.dma_start(raw[:, r, :], stream[bass.ds(index, 1), :, :].rearrange("a p n -> p (a n)")
                         ).then_inc(landed[r], 16)

        def three(out_ap, a_hi, a_lo, wa_hi, wa_lo, start, stop, weights_stay):
            pairs = ((a_hi, wa_hi), (a_lo, wa_hi), (a_hi, wa_lo))
            for i, (a, w) in enumerate(pairs):
                lhs, rhs = (w, a) if weights_stay else (a, w)
                mm = nc.tensor.matmul(out_ap, lhs, rhs, start=start and i == 0, stop=stop and i == 2)
            return mm

        moe = U["moe"]
        MOE0 = unit(moe)

        def moe_unit(p, e, k):
            q, r = MOE0[0], MOE0[1] + k
            return q + STEPS * (E * p) + STEPS * e + r // RING, r % RING

        @block.sync
        def _(sp):
            sp.dma_start(tok_b, mem[0].rearrange("(b p) d -> p b d", p=P)).then_inc(s_mem, 16)
            sp.dma_start(col[:, :], cols).then_inc(s_col, 16)
            sp.dma_start(res[:, :, :], x[0].rearrange("(b p) d -> p b d", p=P)).then_inc(s_in, 16)
            for n in range(moe):
                load(sp, unit(n), n)
                if n == U["pw1"] + RING - 1:
                    sp.wait_ge(s_turn, NC * (TURN["mix1"] + 1))
                    sp.dma_start(tok_c, mem[0].rearrange("(b p) d -> p b d", p=P)).then_inc(s_mem2, 16)

            def experts(p):
                with sp.Fori(0, E * STEPS) as i:
                    for k in range(RING):
                        q, r = plus(MOE0, k)
                        load(sp, (q + E * STEPS * p + i, r), i * RING + (moe + k))

            experts(0)
            sp.wait_ge(s_over, 1)
            flag = sp.value_load(over_i[0:1, 0:1], min_val=0, max_val=1)
            with sp.If(flag > 0):
                experts(1)
            sp.wait_ge(s_fin, NB)
            sp.dma_start(out[0].rearrange("(b p) d -> p b d", p=P), res[:, :, :]).then_inc(s_out, 16)
            sp.wait_ge(s_out, 16)

        @block.gpsimd
        def _(pool):
            def split_lo(u):
                q, r = u
                pool.wait_ge(s_hi, RING * q + (r + 1))
                nc.gpsimd.tensor_tensor(w_lo[:, r % SPLIT, SHARE:], raw[:, r, SHARE:], w_hi[:, r % SPLIT, SHARE:].bitcast(F32),
                                        ALU.subtract).then_inc(s_lo_p, 1)

            def split_next(n):
                while unit_at[0] < n:
                    split_lo(unit(unit_at[0]))
                    unit_at[0] += 1

            unit_at = [0]

            def load_row(i):
                pool.dma_start(row[:, i % ROW_SLOTS, :], rows[i:i + 1, :].partition_broadcast(P)
                               ).then_inc(s_row[i % ROW_SLOTS], 16)

            nc.gpsimd.memset(eps[:, :], EPS).then_inc(s_const, 1)
            nc.gpsimd.memset(ident[:, :], 0.0).then_inc(s_zero, 1)
            nc.gpsimd.memset(ones[:, :], 1.0).then_inc(s_zero, 1)
            pool.wait_ge(s_zero, 2)
            nc.gpsimd.affine_select(out=ident[:, :], in_=ident[:, :], compare_op=ALU.not_equal, fill=1.0, base=0,
                                    pattern=[[-1, P]], channel_multiplier=1).then_inc(s_const, 1)
            for i in range(ROW_SLOTS):
                load_row(i)
            nc.gpsimd.affine_select(out=upper[:, :], in_=ones[:, :], compare_op=ALU.is_gt, fill=0.0, base=0,
                                    pattern=[[1, P]], channel_multiplier=-1).then_inc(s_const, 1)
            nc.gpsimd.iota(iota[:, :], [[1, SLOTS]], base=0, channel_multiplier=0,
                           allow_small_or_imprecise_dtypes=True).then_inc(s_const, 1)
            nc.gpsimd.iota(rank[:, :], [[-1, E]], base=E, channel_multiplier=0,
                           allow_small_or_imprecise_dtypes=True).then_inc(s_const, 1)
            split_next(U["pool"] + 3)
            pool.wait_ge(s_pd, NC)
            load_row(3)
            pool.wait_ge(s_pb, 2 * NB)
            load_row(4)
            load_row(5)
            pool.wait_ge(s_t, NB)
            load_row(6)
            split_next(U["ffn"] + 3)
            pool.wait_ge(s_t, 2 * NB)
            load_row(7)
            split_next(U["pw1"] + 3)
            pool.wait_ge(s_t, 3 * NB)
            load_row(8)
            split_next(U["q1"] + 3)
            pool.wait_ge(s_p2, NB)
            load_row(9)
            split_next(moe)

            def experts(p):
                with pool.Fori(0, E * STEPS) as i:
                    for k in range(RING):
                        q, r = plus(MOE0, k)
                        split_lo((q + E * STEPS * p + i, r))

            experts(0)
            pool.wait_ge(s_over, 1)
            flag = pool.value_load(over_i[0:1, 0:1], min_val=0, max_val=1)
            with pool.If(flag > 0):
                experts(1)

        @block.scalar
        def _(act):
            at = [0]

            def ahead(n):
                while at[0] < min(n, moe):
                    split_hi(act, unit(at[0]))
                    at[0] += 1

            def statistics(name, src, junk, updated=None):
                i = STAT[name]
                for b in range(NB):
                    if updated is not None:
                        act.wait_ge(s_res, NB * RES[updated] + b + 1)
                    nc.scalar.activation(junk[:, b, :], src[:, b, :], ACT.Square,
                                         accum_out=stat[:, 0, i, b:b + 1]).then_inc(s_sq, 1)

            def chunks_out(turn, gain_name, bank0=4):
                for c in range(NC):
                    act.wait_ge(s_turn, NC * TURN[turn] + (c | 1) + 1)
                    nc.scalar.activation(xth[:, c, :], turned(bank0, c), ACT.Copy, scale=gain(gain_name, c)
                                         ).then_inc(s_xth, 1)

            def chan_result(dst, s_mine, n0):
                for c in range(NC):
                    ahead(n0 + c // 2 + 1 + SPLIT)
                    act.wait_ge(s_used, n0 + c // 2 + 1)
                    nc.scalar.copy(dst[:, c, :], ps[:, 4 + c % 4, 0:S]).then_inc(s_mine, 1)

            def values_out(n0):
                for n in range(2):
                    ahead(n0 + 2 * n + 2 + SPLIT)
                    act.wait_ge(s_used, n0 + 2 * n + 2)
                    for b in range(NB):
                        nc.scalar.copy(buf_v[:, b, n * NT:n * NT + NT], y_ps[:, b, n, :]).then_inc(s_vc, 1)

            def attention(layer):
                n0 = U[f"q{layer}"]
                ahead(n0 + SPLIT)
                statistics(f"xa{layer}", res, tok_b, f"mix{layer}")
                chunks_out(f"xa{layer}", f"xa{layer}")
                chan_result(chan_a, s_qc, n0)
                ahead(n0 + 4 + SPLIT)
                for h in range(HEADS):
                    for b in range(NB):
                        i = h * NB + b
                        act.wait_ge(s_nm, HEADS * layer + h + 1)
                        nc.scalar.activation(chan_b[:, i, :], ps[:, 4 + h, b * S:b * S + S], ACT.Exp,
                                             bias=soft[:, 1, i:i + 1], scale=SCALE,
                                             accum_out=soft[:, 2, i:i + 1]).then_inc(s_ex, 1)
                for h in range(0, HEADS, 2):
                    act.wait_ge(s_pt, HEADS * layer + h + 1)
                    nc.scalar.copy(buf_c[:, h * 2 * S:(h + 1) * 2 * S], ps[:, 4 + h, :]).then_inc(s_pte, 1)
                for c in range(NC):
                    act.wait_ge(s_ov, NC * layer + (c | 1) + 1)
                    nc.scalar.copy(xth[:, c, :], turned(4, c)).then_inc(s_xth, 1)
                ahead(U[f"o{layer}"] + 4 + SPLIT)
                act.wait_ge(s_used, U[f"o{layer}"] + 4)
                statistics(f"post_xa{layer}", y_tok, tok_b)

            act.wait_ge(s_const, 1)
            act.wait_ge(s_mem, 16)
            statistics("mem", tok_b, tok_c)
            act.wait_ge(s_in, 16)
            act.wait_ge(s_xn, NB)
            statistics("mix0", res, tok_b)
            act.wait_ge(s_col, 16)
            chunks_out("mem", "mem")
            for c in range(NC):
                act.wait_ge(s_turn, NC * TURN["mix0"] + (c | 1) + 1)
                nc.scalar.activation(pool_a[:, c, PAD:PAD + S], turned(0, c), ACT.Copy, scale=gain("mix0", c)
                                     ).then_inc(s_f0, 1)
            chan_result(buf_k, s_kc, U["k0"])
            values_out(U["v0"])
            act.wait_ge(s_used, U["pool"])
            for c in range(NC):
                act.wait_ge(s_pd, c + 1)
                nc.scalar.copy(xth[:, c, :], pooled(c)).then_inc(s_xth, 1)
            ahead(U["pool"] + 1 + SPLIT)
            act.wait_ge(s_pb, 2 * NB)
            statistics("post_mix0", tok_b, tok_a)
            attention(0)

            ahead(U["ffn"] + SPLIT)
            statistics("ffn0", res, tok_b, "xa0")
            chunks_out("ffn0", "ffn0", 0)

            def hidden_silu(j, s_silu_, s_ht_, nb, bank, u_gate):
                wait_used(act, u_gate, -1)
                wait_step(act, s_ht_, j)
                nc.scalar.activation(buf_c[:, 0:nb * NT], ps[:, bank:bank + nb, :].rearrange("p b n -> p (b n)"), ACT.Silu
                                     ).then_inc(s_silu_, 1)

            def hidden_hi(j, par, s_ht_, s_hth_, dst, src):
                wait_step(act, s_ht_, j + 1)
                nc.scalar.copy(dst, src).then_inc(s_hth_, 1)

            def step(j, par, u0, first, dense, before=None, last=None):
                if dense:
                    sems, nb, bank = (s_silu, s_ht, s_hth), NB, 4
                    dst, src = hn_hi[:, par * 1024:par * 1024 + 1024], ps[:, 4:6, :].rearrange("p b n -> p (b n)")
                else:
                    sems, nb, bank = (m_silu, m_ht, m_hth), 1, 2
                    dst, src = xt_hi[:, 1024 + par * NT:1024 + par * NT + NT], ps[:, 4, :]
                if first:
                    split_hi(act, plus(u0, 3))
                    if before is not None:
                        gated(before)
                    split_hi(act, plus(u0, 4))
                    hidden_silu(j, sems[0], sems[1], nb, bank, u0)
                    split_hi(act, plus(u0, 5))
                    return (j, par, sems[1], sems[2], dst, src)
                for k in (2, 3, 4):
                    split_hi(act, plus(u0, k))
                hidden_silu(j, sems[0], sems[1], nb, bank, u0)
                split_hi(act, plus(u0, 5))
                if last is not None:
                    gathered(last)
                split_hi(act, plus(u0, 6))
                hidden_hi(j, par, sems[1], sems[2], dst, src)
                split_hi(act, plus(u0, 7))

            u0 = unit(U["ffn"])
            hidden_hi(*step(0, 0, u0, True, True))
            with act.Fori(0, STEPS // 2) as i:
                for d in range(2):
                    f = plus(u0, 4 + 6 * d)
                    step(2 * i + (1 + d), (1 + d) % 2, (f[0] + 2 * i, f[1]), False, True)
            at[0] = U["pw1"]
            ahead(U["pw1"] + SPLIT)
            act.wait_ge(s_used, U["pw1"])
            statistics("post_ffn0", y_tok, tok_b)

            statistics("mix1", res, tok_b, "ffn0")
            chunks_out("mix1", "mix1")
            for c in range(NC):
                ahead(U["pw1"] + c + 1 + SPLIT)
                act.wait_ge(s_used, U["pw1"] + c + 1)
                if c >= 2:
                    act.wait_ge(s_u, c - 1)
                nc.scalar.activation(sg_glu[:, c % 2, :], ps[:, 5 + 2 * (c % 2), 0:S], ACT.Sigmoid,
                                     bias=gain("pw1_b", NC + c)).then_inc(s_sg, 1)
            chunks_out("mem_again", "mem", 0)
            chan_result(buf_k, s_kc, U["k1"])
            act.wait_ge(s_u, NC)
            values_out(U["v1"])
            act.wait_ge(s_xc, 1)
            nc.scalar.activation(chan_c, chan_b, ACT.Square).then_inc(s_vq, 1)
            act.wait_ge(s_ln, 2)
            nc.scalar.activation(ln_row[:, 1, :], ps[:, 5, 0:S], ACT.Sqrt, scale=1.0 / D, bias=eps[:, 0:1]).then_inc(s_vs, 1)
            act.wait_ge(s_ly, 1)
            for c in range(NC):
                nc.scalar.activation(chan_c[:, c, :], chan_b[:, c, :], ACT.Silu, scale=gain("ln_g", c), bias=gain("ln_b", c)
                                     ).then_inc(s_z, 1)
            for c in range(NC):
                act.wait_ge(s_z, c + 1)
                nc.scalar.copy(xth[:, c, :], chan_c[:, c, :]).then_inc(s_xth, 1)
            ahead(U["pw2"] + 4 + SPLIT)
            act.wait_ge(s_p2, NB)
            statistics("post_mix1", tok_a, tok_c)
            attention(1)

            statistics("ffn1", res, tok_b, "xa1")
            for b in range(NB):
                act.wait_ge(s_xn, NB * TURN["ffn1"] + b + 1)
                nc.scalar.copy(hn_hi[:, b * D:b * D + D], tok_c[:, b, :]).then_inc(s_hnh, 1)
            for c in range(NC):
                act.wait_ge(s_turn, NC * TURN["ffn1"] + (c | 1) + 1)
                nc.scalar.activation(chan_a[:, c, :], turned(4, c), ACT.Copy, scale=gain("ffn1", c)).then_inc(s_rf, 1)
            act.wait_ge(s_e2, 1)
            nc.scalar.activation(rtmp[:, 5, :], rtmp[:, 4, :], ACT.Exp).then_inc(s_e2x, 1)

            def gathered(idx):
                for c in range(NC):
                    act.wait_ge(s_gath, 2 * idx + c // 4 + 1)
                    nc.scalar.activation(xt_hi[:, c * P:c * P + P], ps[:, 5 + c // 4, (c % 4) * P:(c % 4) * P + P], ACT.Copy,
                                         scale=gain("ffn1", c)).then_inc(s_xth, 1)

            def gated(idx):
                for n in range(2):
                    nc.scalar.activation(ys_hi[:, n * NT:n * NT + NT], ps[:, n, :], ACT.Copy, scale=slot_gate[:, 0:1]
                                         ).then_inc(s_ysh, 1)

            def experts(p):
                nc.scalar.activation(silu_at[:, :], eps[:, :], ACT.Silu).then_inc(s_tab, 1)
                gathered(9 * p)
                with act.Fori(0, E) as e:
                    u0 = moe_unit(p, e, 0)
                    for k in range(3):
                        split_hi(act, plus(u0, k))
                    wait_used(act, u0, 1)
                    act.wait_ge(s_gs, E * p + e + 1)
                    late = step(E * STEPS * p + STEPS * e, 0, u0, True, False, before=9 * p + e)
                    act.wait_ge(s_gtp, E * p + e + 1)
                    nc.scalar.copy(sel_t[:, :], ps[:, 7, 0:NB * SLOTS]).then_inc(s_gt, 1)
                    hidden_hi(*late)
                    with act.Fori(0, STEPS // 2 - 1) as i:
                        for d in range(2):
                            f = plus(u0, 4 + 6 * d)
                            step(E * STEPS * p + STEPS * e + 2 * i + (1 + d), (1 + d) % 2, (f[0] + 2 * i, f[1]), False, False)
                    for j in (STEPS - 2, STEPS - 1):
                        step(E * STEPS * p + STEPS * e + j, j % 2, plus(u0, 6 * j - 2), False, False,
                             last=9 * p + e + 1 if j == STEPS - 1 else None)
                wait_used(act, moe_unit(p, E, 0), 1)
                act.wait_ge(s_gs, E * (p + 1) + 1)
                gated(9 * p + E)

            experts(0)
            act.wait_ge(s_over, 1)
            flag = act.value_load(over_i[0:1, 0:1], min_val=0, max_val=1)
            with act.If(flag > 0):
                experts(1)
            act.wait_ge(s_fin0, 1)
            statistics("post_ffn1", acc, tok_b)

        @block.vector
        def _(dve):
            at = [0]
            chain = [0]

            def ahead(n):
                while at[0] < min(n, moe):
                    split_lo(dve, unit(at[0]))
                    at[0] += 1

            def link(ins):
                chain[0] += 1
                ins.then_inc(s_rt, 1)
                dve.wait_ge(s_rt, chain[0])

            def root_inverse(name):
                i = STAT[name]
                dve.wait_ge(s_sq, NB * (i + 1))
                mean, half, y = (stat[:, k, i, :] for k in range(3))
                link(nc.vector.tensor_scalar(mean, mean, 1.0 / D, EPS, ALU.mult, ALU.add))
                link(nc.vector.tensor_scalar(half.bitcast(I32), mean.bitcast(I32), 1, None, ALU.logical_shift_right))
                link(nc.vector.tensor_scalar(y.bitcast(I32), half.bitcast(I32), -1.0, float(0x5F3759DF), ALU.mult, ALU.add))
                for _ in range(3):
                    link(nc.vector.scalar_tensor_tensor(out=half, in0=y, scalar=-0.5, in1=y, op0=ALU.mult, op1=ALU.mult))
                    link(nc.vector.tensor_tensor(half, half, mean, ALU.mult))
                    link(nc.vector.scalar_tensor_tensor(out=y, in0=half, scalar=1.5, in1=y, op0=ALU.add, op1=ALU.mult))

            def normalise(name, src, dst):
                i = STAT[name]
                for b in range(NB):
                    nc.vector.tensor_scalar(dst[:, b, :], src[:, b, :], stat[:, 2, i, b:b + 1], None, ALU.mult
                                            ).then_inc(s_xn, 1)

            def chunks_rest(xt, gain_name, bank0=4):
                for c in range(NC):
                    dve.wait_ge(s_xth, NC * XT[xt] + (c | 1) + 1)
                    nc.vector.scalar_tensor_tensor(out=xtl[:, c, :], in0=turned(bank0, c), scalar=gain(gain_name, c),
                                                   in1=xth[:, c, :].bitcast(F32), op0=ALU.mult, op1=ALU.subtract
                                                   ).then_inc(s_xtl, 1)

            def add_to_residual(name, src, row_index, t, done=None):
                i = STAT[name]
                k = POST[name]
                dve.wait_ge(s_row[row_index % ROW_SLOTS], 16 * (row_index // ROW_SLOTS + 1))
                for b in range(NB):
                    nc.vector.scalar_tensor_tensor(out=t[:, b, :], in0=src[:, b, :], scalar=stat[:, 2, i, b:b + 1],
                                                   in1=row[:, row_index % ROW_SLOTS, :], op0=ALU.mult, op1=ALU.mult
                                                   ).then_inc(s_t, 1)
                    dve.wait_ge(s_t, NB * k + b + 1)
                    nc.vector.tensor_tensor(res[:, b, :], res[:, b, :], t[:, b, :], ALU.add).then_inc(done or s_res, 1)

            def attention(layer):
                n0 = U[f"q{layer}"]
                ahead(n0 + SPLIT)
                root_inverse(f"xa{layer}")
                normalise(f"xa{layer}", res, tok_c)
                chunks_rest(f"xa{layer}", f"xa{layer}")
                ahead(n0 + 4 + SPLIT)

                def maximum(h):
                    i = slice(h * NB, (h + 1) * NB)
                    dve.wait_ge(s_sc, HEADS * layer + h + 1)
                    link(nc.vector.tensor_reduce(soft[:, 0, i], ps[:, 4 + h, :].rearrange("p (b m) -> p b m", b=NB), AX.X,
                                                 ALU.max))
                    nc.vector.tensor_scalar(soft[:, 1, i], soft[:, 0, i], -SCALE, None, ALU.mult).then_inc(s_nm, 1)

                def probabilities(h):
                    dve.wait_ge(s_ex, NC * layer + NB * (h + 1))
                    link(nc.vector.reciprocal(soft[:, 3, h * NB:(h + 1) * NB], soft[:, 2, h * NB:(h + 1) * NB]))
                    for i in range(h * NB, (h + 1) * NB):
                        nc.vector.tensor_scalar(chan_b[:, i, :], chan_b[:, i, :], soft[:, 3, i:i + 1], None, ALU.mult
                                                ).then_inc(s_pn, 1)

                maximum(0)
                for h in range(1, HEADS):
                    maximum(h)
                    probabilities(h - 1)
                probabilities(HEADS - 1)
                for h in range(1, HEADS, 2):
                    dve.wait_ge(s_pt, HEADS * layer + h + 1)
                    nc.vector.tensor_copy(buf_c[:, h * 2 * S:(h + 1) * 2 * S], ps[:, 4 + h, :]).then_inc(s_pto, 1)
                for c in range(NC):
                    dve.wait_ge(s_xth, NC * XT[f"o{layer}"] + (c | 1) + 1)
                    nc.vector.tensor_tensor(xtl[:, c, :], turned(4, c), xth[:, c, :].bitcast(F32), ALU.subtract
                                            ).then_inc(s_xtl, 1)
                ahead(U[f"o{layer}"] + 4 + SPLIT)
                root_inverse(f"post_xa{layer}")
                add_to_residual(f"post_xa{layer}", y_tok, 4 + 4 * layer, tok_c)

            nc.vector.memset(zeros[:, :].bitcast(F32), 0.0).then_inc(s_init, 1)
            for s in m_steps:
                dve.sem_inc(s, 1)
            nc.vector.memset(sel_t[:, :].bitcast(F32), 0.0).then_inc(s_gt, 1)
            nc.vector.memset(slot_gate[:, :], 0.0).then_inc(s_gs, 1)
            nc.vector.memset(place[:, :, :], -1.0).then_inc(s_init, 1)
            nc.vector.memset(gate[:, :, :], 0.0).then_inc(s_init, 1)
            root_inverse("mem")
            normalise("mem", tok_b, tok_a)
            root_inverse("mix0")
            normalise("mix0", res, tok_c)
            dve.wait_ge(s_col, 16)
            chunks_rest("mem", "mem")
            dve.wait_ge(s_turn, NC)
            nc.vector.memset(pool_a[:, :, 0:PAD], 0.0).then_inc(s_pad, 1)
            ahead(U["k0"] + 5)
            dve.wait_ge(s_f0, NC)
            dve.wait_ge(s_turn, 2 * NC)
            dve.wait_ge(s_pad, 1)
            src, lead = pool_a, 0
            for g, w in enumerate(WINDOWS):
                c0, lead = 2 * g, lead + w // 2
                dst = (pool_b, pool_c)[g % 2]
                nc.vector.tensor_tensor(dst[:, c0:NC, lead:], src[:, c0:NC, lead:], src[:, c0:NC, lead - w // 2:PAD + S - w // 2],
                                        ALU.add).then_inc(s_win, 1)
                dve.wait_ge(s_win, g + 1)
                src = dst
            dve.wait_ge(s_row[0], 16)
            for c in range(NC):
                p_c = pooled(c)
                nc.vector.tensor_tensor(p_c, p_c, row[:, 0, (c // 2) * S:(c // 2 + 1) * S], ALU.mult).then_inc(s_win, 1)
            for c in range(NC):
                p_c = pooled(c)
                dve.wait_ge(s_win, len(WINDOWS) + c + 1)
                nc.vector.tensor_tensor(p_c, p_c, pool_a[:, c, PAD:PAD + S], ALU.subtract).then_inc(s_pd, 1)
            ahead(U["pool"])
            for c in range(NC):
                dve.wait_ge(s_xth, NC * XT["pooled"] + c + 1)
                nc.vector.tensor_tensor(xtl[:, c, :], pooled(c), xth[:, c, :].bitcast(F32), ALU.subtract
                                        ).then_inc(s_xtl, 1)
            ahead(U["pool"] + 1 + SPLIT)
            dve.wait_ge(s_used, U["pool"] + 1)
            for r, op in ((1, ALU.add), (2, ALU.mult)):
                dve.wait_ge(s_row[r], 16)
                for b in range(NB):
                    if r == 1:
                        nc.vector.tensor_tensor(tok_b[:, b, :], y_tok[:, b, :], row[:, r, :], op).then_inc(s_pb, 1)
                    else:
                        dve.wait_ge(s_pb, b + 1)
                        nc.vector.tensor_tensor(tok_b[:, b, :], tok_b[:, b, :], row[:, r, :], op).then_inc(s_pb, 1)
            root_inverse("post_mix0")
            add_to_residual("post_mix0", tok_b, 3, tok_c)
            attention(0)

            ahead(U["ffn"] + SPLIT)
            root_inverse("ffn0")
            normalise("ffn0", res, tok_c)
            chunks_rest("ffn0", "ffn0", 0)

            def hidden_mul(j, s_silu_, s_mul_, nb, bank, u_up):
                wait_step(dve, s_silu_, j + 1)
                wait_used(dve, u_up, -1)
                h = buf_c[:, 0:nb * NT]
                nc.vector.tensor_tensor(h, h, ps[:, bank:bank + nb, :].rearrange("p b n -> p (b n)"), ALU.mult
                                        ).then_inc(s_mul_, 1)

            def hidden_lo(j, s_hth_, s_htl_, dst, src, high):
                wait_step(dve, s_hth_, j + 1)
                nc.vector.tensor_tensor(dst, src, high.bitcast(F32), ALU.subtract).then_inc(s_htl_, 1)

            def step(j, par, u0, first, dense, before=None, last=None):
                if dense:
                    sems, nb, bank = (s_silu, s_mul, s_hth, s_htl), NB, 6
                    a, n = par * 1024, 1024
                    dst, high, src = hn_lo[:, a:a + n], hn_hi[:, a:a + n], ps[:, 4:6, :].rearrange("p b n -> p (b n)")
                else:
                    sems, nb, bank = (m_silu, m_mul, m_hth, m_htl), 1, 3
                    a, n = 1024 + par * NT, NT
                    dst, high, src = xt_lo[:, a:a + n], xt_hi[:, a:a + n], ps[:, 4, :]
                late = (j, sems[2], sems[3], dst, src, high)
                if first:
                    split_lo(dve, plus(u0, 3))
                    if before is not None:
                        gated(*before)
                    split_lo(dve, plus(u0, 4))
                    hidden_mul(j, sems[0], sems[1], nb, bank, plus(u0, 2))
                    split_lo(dve, plus(u0, 5))
                    return late
                for k in (2, 3, 4, 5):
                    split_lo(dve, plus(u0, k))
                hidden_mul(j, sems[0], sems[1], nb, bank, plus(u0, 2))
                if last is not None:
                    gathered(last)
                split_lo(dve, plus(u0, 6))
                hidden_lo(*late)
                split_lo(dve, plus(u0, 7))

            u0 = unit(U["ffn"])
            hidden_lo(*step(0, 0, u0, True, True))
            with dve.Fori(0, STEPS // 2) as i:
                for d in range(2):
                    f = plus(u0, 4 + 6 * d)
                    step(2 * i + (1 + d), (1 + d) % 2, (f[0] + 2 * i, f[1]), False, True)
            at[0] = U["pw1"]
            ahead(U["pw1"] + SPLIT)
            root_inverse("post_ffn0")
            add_to_residual("post_ffn0", y_tok, 5, tok_c)

            root_inverse("mix1")
            normalise("mix1", res, tok_c)
            chunks_rest("mix1", "mix1")
            nc.vector.memset(conv_u[:, :, 0:CPAD], 0.0).then_inc(s_pad, 1)

            def gated_unit(c):
                dve.wait_ge(s_sg, c + 1)
                nc.vector.scalar_tensor_tensor(out=conv_u[:, c, CPAD:], in0=ps[:, 4 + 2 * (c % 2), 0:S], scalar=gain("pw1_b", c),
                                               in1=sg_glu[:, c % 2, :], op0=ALU.add, op1=ALU.mult).then_inc(s_u, 1)

            def taps(c):
                done = TAPS * c
                for j in range(TAPS):
                    for i in range(2):
                        w = col[:, COL["dw_w"] + j * NC + c + i:COL["dw_w"] + j * NC + c + i + 1]
                        v, u = chan_b[:, c + i, :], conv_u[:, c + i, j:j + S]
                        if j == 0:
                            ins = nc.vector.tensor_scalar(v, u, w, gain("dw_b", c + i), ALU.mult, ALU.add)
                        else:
                            dve.wait_ge(s_cv, done + 2 * j + i - 1)
                            ins = nc.vector.scalar_tensor_tensor(out=v, in0=u, scalar=w, in1=v, op0=ALU.mult, op1=ALU.add)
                        ins.then_inc(s_cv, 1)

            for c in range(NC):
                ahead(U["pw1"] + c + 1 + SPLIT)
                gated_unit(c)
                if c == 1:
                    dve.wait_ge(s_mem2, 16)
                    nc.vector.tensor_scalar(tok_c[:, 0, :], tok_c[:, 0, :], stat[:, 2, STAT["mem"], 0:1], None, ALU.mult).then_inc(s_xn, 1)
                    nc.vector.tensor_scalar(tok_c[:, 1, :], tok_c[:, 1, :], stat[:, 2, STAT["mem"], 1:2], None, ALU.mult).then_inc(s_xn, 1)
            dve.wait_ge(s_pad, 2)
            dve.wait_ge(s_u, NC)
            chunks_rest("mem_again", "mem", 0)
            ahead(U["k1"] + 3)
            for c in range(0, NC, 2):
                taps(c)
                ahead(U["k1"] + SPLIT + 2 * (c // 2 + 1))
            dve.wait_ge(s_ln, 1)
            nc.vector.tensor_scalar(ln_row[:, 0, :], ps[:, 4, 0:S], -1.0 / D, None, ALU.mult).then_inc(s_mu, 1)
            dve.wait_ge(s_mu, 1)
            dve.wait_ge(s_cv, TAPS * NC)
            nc.vector.tensor_tensor(chan_b, chan_b, ln_row[:, 0:1, :].broadcast_to([P, NC, S]), ALU.add).then_inc(s_xc, 1)
            dve.wait_ge(s_vs, 1)
            dve.wait_ge(s_xc, 1)
            nc.vector.reciprocal(ln_row[:, 0, :], ln_row[:, 1, :]).then_inc(s_mu, 1)
            dve.wait_ge(s_mu, 2)
            nc.vector.tensor_tensor(chan_b, chan_b, ln_row[:, 0:1, :].broadcast_to([P, NC, S]), ALU.mult).then_inc(s_ly, 1)
            for c in range(NC):
                dve.wait_ge(s_xth, NC * XT["z"] + c + 1)
                nc.vector.tensor_tensor(xtl[:, c, :], chan_c[:, c, :], xth[:, c, :].bitcast(F32), ALU.subtract).then_inc(s_xtl, 1)
            ahead(U["pw2"] + 4 + SPLIT)
            dve.wait_ge(s_used, U["pw2"] + 4)
            dve.wait_ge(s_row[0], 48)
            for b in range(NB):
                nc.vector.tensor_tensor(tok_a[:, b, :], y_tok[:, b, :], row[:, 0, :], ALU.add).then_inc(s_p2, 1)
            root_inverse("post_mix1")
            add_to_residual("post_mix1", tok_a, 7, tok_b)
            attention(1)

            root_inverse("ffn1")
            normalise("ffn1", res, tok_c)
            for b in range(NB):
                dve.wait_ge(s_hnh, b + 1)
                h = slice(b * D, b * D + D)
                nc.vector.tensor_tensor(hn_lo[:, h], tok_c[:, b, :], hn_hi[:, h].bitcast(F32), ALU.subtract).then_inc(s_hnl, 1)
            lg, eq, key1, key2, rest, g1, g2, chosen = (route[:, i, :, :] for i in range(8))
            top1, best, top2, best2, diff, expd, w1, w2 = (rtmp[:, i, :] for i in range(8))
            dve.wait_ge(s_const, 5)
            dve.wait_ge(s_init, 3)
            dve.wait_ge(s_lg, 1)
            link(nc.vector.tensor_copy(route[:, 0, :, :].rearrange("p b e -> p (b e)"), ps[:, 0, 0:NB * E]))
            for vals, top, b_, key in ((lg, top1, best, key1), (rest, top2, best2, key2)):
                link(nc.vector.tensor_reduce(top, vals, AX.X, ALU.max))
                for b in range(NB):
                    link(nc.vector.tensor_scalar(eq[:, b, :], vals[:, b, :], top[:, b:b + 1], None, ALU.is_equal))
                    link(nc.vector.tensor_tensor(eq[:, b, :], eq[:, b, :], rank[:, :], ALU.mult))
                link(nc.vector.tensor_reduce(b_, eq, AX.X, ALU.max))
                for b in range(NB):
                    link(nc.vector.tensor_scalar(key[:, b, :], eq[:, b, :], b_[:, b:b + 1], None, ALU.is_equal))
                if vals is lg:
                    link(nc.vector.scalar_tensor_tensor(out=rest, in0=key1, scalar=-BIG, in1=lg, op0=ALU.mult, op1=ALU.add))
            link(nc.vector.tensor_tensor(chosen, key1, key2, ALU.add))
            nc.vector.tensor_tensor(diff, top2, top1, ALU.subtract).then_inc(s_e2, 1)
            nc.vector.tensor_copy(route[:, 8, :, :], chosen).then_inc(s_sel, 1)
            dve.wait_ge(s_e2x, 1)
            link(nc.vector.tensor_scalar(w2, expd, 1.0, None, ALU.add))
            link(nc.vector.reciprocal(w1, w2))
            link(nc.vector.tensor_tensor(w2, expd, w1, ALU.mult))
            for b in range(NB):
                link(nc.vector.tensor_scalar(g1[:, b, :], key1[:, b, :], w1[:, b:b + 1], None, ALU.mult))
                link(nc.vector.scalar_tensor_tensor(out=gate[:, 0:E, b], in0=key2[:, b, :], scalar=w2[:, b:b + 1],
                                                    in1=g1[:, b, :], op0=ALU.mult, op1=ALU.add))
            dve.wait_ge(s_pos, 1)
            link(nc.vector.tensor_scalar(g2.rearrange("p b e -> p (b e)"), ps[:, 0, 64:64 + NB * E], 1.0, None, ALU.add))
            link(nc.vector.tensor_tensor(g2, g2, chosen, ALU.mult))
            link(nc.vector.tensor_scalar(place[:, 0:E, :].rearrange("p e b -> p b e"), g2, -1.0, None, ALU.add))
            link(nc.vector.tensor_scalar(place2[:, :, :], place[:, :, :], -float(SLOTS), None, ALU.add))
            link(nc.vector.tensor_reduce(over[:, :], ps[:, 0, 128:128 + E], AX.X, ALU.max))
            nc.vector.tensor_scalar(over_i[:, :], over[:, :], float(SLOTS) + 0.5, None, ALU.is_gt).then_inc(s_over, 1)
            nc.vector.memset(acc, 0.0).then_inc(s_acc, 1)

            def select(where, e):
                for b in range(NB):
                    nc.vector.tensor_scalar(sel[:, b * SLOTS:(b + 1) * SLOTS], iota[:, :],
                                            where[:, bass.ds(e, 1), b], None, ALU.is_equal).then_inc(s_g, 1)

            def gathered(idx):
                for c in range(NC):
                    dve.wait_ge(s_xth, NC * (XT["gather"] + idx) + ((c | 3) + 1))
                    o = slice(c * P, c * P + P)
                    nc.vector.scalar_tensor_tensor(out=xt_lo[:, o], in0=ps[:, 5 + c // 4, (c % 4) * P:(c % 4) * P + P],
                                                   scalar=gain("ffn1", c), in1=xt_hi[:, o].bitcast(F32), op0=ALU.mult,
                                                   op1=ALU.subtract).then_inc(s_xtl, 1)

            def gated(idx, count):
                dve.wait_ge(s_gs, count)
                for n in range(2):
                    dve.wait_ge(s_ysh, 2 * idx + n + 1)
                    o = slice(n * NT, n * NT + NT)
                    nc.vector.scalar_tensor_tensor(out=ys_lo[:, o], in0=ps[:, n, :], scalar=slot_gate[:, 0:1],
                                                   in1=ys_hi[:, o].bitcast(F32), op0=ALU.mult, op1=ALU.subtract
                                                   ).then_inc(s_ysl, 1)

            def combined(idx):
                dve.wait_ge(s_acc, 4 * idx + 1)
                for i, bank in enumerate(COMBINE_BANKS):
                    dve.wait_ge(s_comb, 4 * idx + i + 1)
                    a = acc[:, i // 2, (i % 2) * NT:(i % 2) * NT + NT]
                    nc.vector.tensor_tensor(a, a, ps[:, bank, :], ALU.add).then_inc(s_acc, 1)

            def experts(p):
                where = (place, place2)[p]
                select(where, 0)
                gathered(9 * p)
                with dve.Fori(0, E) as e:
                    u0 = moe_unit(p, e, 0)
                    for k in range(3):
                        split_lo(dve, plus(u0, k))
                    late = step(E * STEPS * p + STEPS * e, 0, u0, True, False, before=(9 * p + e, E * p + e + 1))
                    combined(9 * p + e)
                    dve.wait_ge(s_gt, E * p + e + 2)
                    nc.vector.tensor_copy(slot_gate[:, :], ps[:, 7, 2 * SLOTS:2 * SLOTS + 1]).then_inc(s_gs, 1)
                    hidden_lo(*late)
                    select(where, e + 1)
                    with dve.Fori(0, STEPS // 2 - 1) as i:
                        for d in range(2):
                            f = plus(u0, 4 + 6 * d)
                            step(E * STEPS * p + STEPS * e + 2 * i + (1 + d), (1 + d) % 2, (f[0] + 2 * i, f[1]), False, False)
                    for j in (STEPS - 2, STEPS - 1):
                        step(E * STEPS * p + STEPS * e + j, j % 2, plus(u0, 6 * j - 2), False, False,
                             last=9 * p + e + 1 if j == STEPS - 1 else None)
                gated(9 * p + E, E * (p + 1) + 1)
                combined(9 * p + E)
                dve.wait_ge(s_acc, 4 * (9 * p + E + 1) + 1)

            experts(0)
            flag = dve.value_load(over_i[0:1, 0:1], min_val=0, max_val=1)
            with dve.If(flag > 0):
                experts(1)
            nc.vector.memset(over[:, :], 0.0).then_inc(s_fin0, 1)
            root_inverse("post_ffn1")
            add_to_residual("post_ffn1", acc, 9, tok_c, s_fin)

        @block.tensor
        def _(pe):
            def turn(name, src, bank0=4):
                pe.wait_ge(s_xn, NB * (TURN[name] + 1))
                for c in range(NC):
                    for b in range(NB):
                        mm = nc.tensor.transpose(turned(bank0, c)[:, b * P:(b + 1) * P], src[:, b, c * P:(c + 1) * P], ident[:, :])
                    mm.then_inc(s_turn, 1)

            def have_chunk(xt, k, per):
                if xt is not None and k % per == 0:
                    pe.wait_ge(s_xtl, NC * xt + (k + per))

            def chan_unit(n, banks, xt=None):
                q, r = unit(n)
                wait_low(pe, (q, r))
                for i, bank in enumerate(banks):
                    for k in range(NC):
                        have_chunk(xt if i == 0 else None, k, 2)
                        o = slice((i * NC + k) * P, (i * NC + k + 1) * P)
                        mm = three(ps[:, bank, 0:S], xth[:, k, :], xtl[:, k, :], w_hi[:, r % SPLIT, o], w_lo[:, r % SPLIT, o],
                                   k == 0, k == NC - 1, True)
                mm.then_inc(s_used, 1)

            def chan_product(n0, s_copied, first, xt):
                for i in range(4):
                    if i >= 2:
                        pe.wait_ge(s_copied, first + 2 * (i - 1))
                    chan_unit(n0 + i, (4 + 2 * i % 4, 5 + 2 * i % 4), XT[xt] if i == 0 else None)

            def tok_product(n0, xt=None):
                for n in range(2):
                    for half in range(2):
                        q, r = unit(n0 + 2 * n + half)
                        wait_low(pe, (q, r))
                        for k in range(4):
                            kk = 4 * half + k
                            o = slice(k * NT, (k + 1) * NT)
                            have_chunk(XT[xt] if xt and n == 0 else None, kk, 2)
                            for b in range(NB):
                                t = slice(b * P, (b + 1) * P)
                                mm = three(y_ps[:, b, n, :], xth[:, kk, t], xtl[:, kk, t], w_hi[:, r % SPLIT, o],
                                           w_lo[:, r % SPLIT, o], kk == 0, kk == NC - 1, False)
                        mm.then_inc(s_used, 1)

            def have_xt(name):
                pe.wait_ge(s_xtl, NC * (XT[name] + 1))

            def attention(layer):
                turn(f"xa{layer}", tok_c)
                chan_product(U[f"q{layer}"], s_qc, NC * layer, f"xa{layer}")
                pe.wait_ge(s_qc, NC * (layer + 1))
                pe.wait_ge(s_kc, NC * (layer + 1))
                for h in range(HEADS):
                    for b in range(NB):
                        for d in range(2):
                            mm = nc.tensor.matmul(ps[:, 4 + h, b * S:(b + 1) * S], chan_a[:, 2 * h + d, b * P:(b + 1) * P],
                                                  buf_k[:, 2 * h + d, :], start=d == 0, stop=d == 1)
                    mm.then_inc(s_sc, 1)
                for h in range(HEADS):
                    pe.wait_ge(s_pn, NC * layer + NB * (h + 1))
                    for m in range(2):
                        for b in range(NB):
                            mm = nc.tensor.transpose(ps[:, 4 + h, m * S + b * P:m * S + (b + 1) * P],
                                                     chan_b[:, h * NB + b, m * P:(m + 1) * P], ident[:, :])
                    mm.then_inc(s_pt, 1)
                pe.wait_ge(s_vc, 4 * (layer + 1))
                for h in range(HEADS):
                    pe.wait_ge((s_pte, s_pto)[h % 2], 2 * layer + h // 2 + 1)
                    for d in range(2):
                        for m in range(2):
                            mm = nc.tensor.matmul(turned(4, 2 * h + d), buf_v[:, m, (2 * h + d) * P:(2 * h + d + 1) * P],
                                                  buf_c[:, (2 * h + m) * S:(2 * h + m + 1) * S], start=m == 0, stop=m == 1)
                        mm.then_inc(s_ov, 1)
                tok_product(U[f"o{layer}"], f"o{layer}")

            pe.wait_ge(s_const, 2)
            turn("mem", tok_a)
            turn("mix0", tok_c, 0)
            chan_product(U["k0"], s_kc, 0, "mem")
            pe.wait_ge(s_f0, NC)
            tok_product(U["v0"])
            have_xt("pooled")
            pe.wait_ge(s_vc, 4)
            q, r = unit(U["pool"])
            wait_low(pe, (q, r))
            for b in range(NB):
                for g in range(len(WINDOWS)):
                    for k in range(2):
                        c, o = 2 * g + k, slice((2 * g + k) * S, (2 * g + k + 1) * S)
                        t = slice(b * P, (b + 1) * P)
                        mm = three(y_tok[:, b, g * S:(g + 1) * S], xth[:, c, t], xtl[:, c, t], w_hi[:, r % SPLIT, o],
                                   w_lo[:, r % SPLIT, o], k == 0, k == 1, False)
            mm.then_inc(s_used, 1)
            attention(0)

            def clear_y(banks, stop=False):
                for bank in banks:
                    mm = nc.tensor.matmul(ps[:, bank, :], zeros[:, :], zeros[:, None, :].broadcast_to([P, 4, P]),
                                          start=True, stop=stop)
                return mm

            def down(half, par, u, dense, stop=False):
                r = u[1]
                wait_low(pe, u)
                for k in range(2):
                    kk = 2 * half + k
                    for b in range(NB if dense else 1):
                        if dense:
                            o = par * 1024 + kk * S + b * P
                            h_hi, h_lo = hn_hi[:, o:o + P], hn_lo[:, o:o + P]
                        else:
                            o = 1024 + par * NT + kk * P
                            h_hi, h_lo = xt_hi[:, o:o + P], xt_lo[:, o:o + P]
                        for n in range(2):
                            o = slice(k * D + n * NT, k * D + (n + 1) * NT)
                            mm = three(ps[:, 2 * b + n, :], h_hi, h_lo, w_hi[:, r % SPLIT, o], w_lo[:, r % SPLIT, o],
                                       False, stop and k == 1, False)
                mm.then_inc(s_used, 1)

            def hidden(bank, u, dense, xt=None):
                for half in range(2):
                    v = plus(u, half)
                    r = v[1]
                    wait_low(pe, v)
                    for k in range(4):
                        kk, o = 4 * half + k, slice(k * NT, (k + 1) * NT)
                        have_chunk(xt, kk, 2 if dense else 4)
                        for b in range(NB if dense else 1):
                            a = kk * S + b * P if dense else kk * P
                            mm = three(ps[:, bank + b, :], xt_hi[:, a:a + P], xt_lo[:, a:a + P], w_hi[:, r % SPLIT, o],
                                       w_lo[:, r % SPLIT, o], kk == 0, kk == NC - 1, False)
                    mm.then_inc(s_used, 1)

            def turn_hidden(j, dense):
                sm, sh, st = (s_mul, s_htl, s_ht) if dense else (m_mul, m_htl, m_ht)
                wait_step(pe, sm, j + 1)
                wait_step(pe, sh, j)
                for c in range(4):
                    for b in range(NB if dense else 1):
                        o = turned(4, c)[:, b * P:(b + 1) * P] if dense else ps[:, 4, c * P:(c + 1) * P]
                        mm = nc.tensor.transpose(o, buf_c[:, b * NT + c * P:b * NT + (c + 1) * P], ident[:, :])
                mm.then_inc(st, 1)

            def step(j, par, u0, first, dense, xt=None, last=None):
                ss, sm, sh = (s_silu, s_mul, s_htl) if dense else (m_silu, m_mul, m_htl)
                wait_step(pe, sh if dense else ss, j)
                hidden(4 if dense else 2, u0, dense, xt)
                wait_step(pe, sm, j)
                hidden(6 if dense else 3, plus(u0, 2), dense)
                if first:
                    return
                if last is not None:
                    gather(last)
                wait_step(pe, sh, j)
                down(0, 1 - par, plus(u0, 4), dense)
                turn_hidden(j, dense)
                down(1, 1 - par, plus(u0, 5), dense)

            turn("ffn0", tok_c, 0)
            u0 = unit(U["ffn"])
            step(0, 0, u0, True, True, XT["ffn0"])
            pe.wait_ge(s_init, 1)
            clear_y(range(4))
            turn_hidden(0, True)
            with pe.Fori(0, STEPS // 2) as i:
                for d in range(2):
                    f = plus(u0, 4 + 6 * d)
                    step(2 * i + (1 + d), (1 + d) % 2, (f[0] + 2 * i, f[1]), False, True)
            pe.wait_ge(s_htl, STEPS)
            down(0, 0, plus(u0, PER_FFN - 2), True)
            down(1, 0, plus(u0, PER_FFN - 1), True, True)

            turn("mix1", tok_c)
            for c in range(NC):
                if c >= 2:
                    pe.wait_ge(s_u, c - 1)
                chan_unit(U["pw1"] + c, (4 + 2 * (c % 2), 5 + 2 * (c % 2)), XT["mix1"] if c == 0 else None)
            turn("mem_again", tok_c, 0)
            pe.wait_ge(s_u, NC)
            chan_product(U["k1"], s_kc, NC, "mem_again")
            tok_product(U["v1"])
            pe.wait_ge(s_cv, TAPS * NC)
            pe.wait_ge(s_kc, 2 * NC)
            for c in range(NC):
                mm = nc.tensor.matmul(ps[:, 4, 0:S], ones[:, :], chan_b[:, c, :], start=c == 0, stop=c == NC - 1)
            mm.then_inc(s_ln, 1)
            pe.wait_ge(s_vq, 1)
            for c in range(NC):
                mm = nc.tensor.matmul(ps[:, 5, 0:S], ones[:, :], chan_c[:, c, :], start=c == 0, stop=c == NC - 1)
            mm.then_inc(s_ln, 1)
            pe.wait_ge(s_vc, 8)
            tok_product(U["pw2"], "z")
            attention(1)

            turn("ffn1", tok_c)
            pe.wait_ge(s_rf, NC)
            for b in range(NB):
                for c in range(NC):
                    mm = nc.tensor.matmul(ps[:, 0, b * E:(b + 1) * E], chan_a[:, c, b * P:(b + 1) * P],
                                          col[:, COL["router"] + c * E:COL["router"] + (c + 1) * E], start=c == 0, stop=c == NC - 1)
            mm.then_inc(s_lg, 1)
            pe.wait_ge(s_const, 3)
            pe.wait_ge(s_sel, 1)
            chosen = [route[:, 8, b, :] for b in range(NB)]
            nc.tensor.matmul(ps[:, 0, 64:64 + E], upper[:, :], chosen[0], start=True, stop=True)
            nc.tensor.matmul(ps[:, 0, 64 + E:64 + 2 * E], upper[:, :], chosen[1], start=True, stop=False)
            nc.tensor.matmul(ps[:, 0, 64 + E:64 + 2 * E], ones[:, :], chosen[0], start=False, stop=True)
            nc.tensor.matmul(ps[:, 0, 128:128 + E], ones[:, :], chosen[0], start=True, stop=False)
            nc.tensor.matmul(ps[:, 0, 128:128 + E], ones[:, :], chosen[1], start=False, stop=True).then_inc(s_pos, 1)

            def gather(idx):
                pe.wait_ge(s_g, NB * (idx + 1))
                for c in range(NC):
                    for i, (b, part) in enumerate(((0, hn_hi), (0, hn_lo), (1, hn_hi), (1, hn_lo))):
                        mm = nc.tensor.matmul(ps[:, 5 + c // 4, (c % 4) * P:(c % 4 + 1) * P],
                                              part[:, b * D + c * P:b * D + (c + 1) * P], sel[:, b * SLOTS:(b + 1) * SLOTS],
                                              start=i == 0, stop=i == 3)
                    if c % 4 == 3:
                        mm.then_inc(s_gath, 1)

            def combine(idx, transposed):
                pe.wait_ge(s_ysl, 2 * (idx + 1))
                pe.wait_ge(s_gt, transposed + 1)
                for i, bank in enumerate(COMBINE_BANKS):
                    b, n = i // 2, i % 2
                    for part in (ys_hi, ys_lo):
                        mm = nc.tensor.matmul(ps[:, bank, :], sel_t[:, b * P:(b + 1) * P], part[:, n * NT:(n + 1) * NT],
                                              start=part is ys_hi, stop=part is ys_lo)
                    mm.then_inc(s_comb, 1)

            def turn_selection(count, e):
                pe.wait_ge(s_gs, count + 1)
                for b in range(NB):
                    nc.tensor.transpose(ps[:, 7, b * P:(b + 1) * P], sel[:, b * SLOTS:(b + 1) * SLOTS].bitcast(F32), ident[:, :])
                for b in range(NB):
                    mm = nc.tensor.matmul(ps[:, 7, NB * P:NB * P + 1], sel[:, b * SLOTS:(b + 1) * SLOTS].bitcast(F32),
                                          gate[:, bass.ds(e, 1), b], start=b == 0, stop=b == 1)
                mm.then_inc(s_gtp, 1)

            def experts(p):
                if p == 0:
                    pe.wait_ge(s_over, 1)
                    pe.wait_ge(s_hnl, NB)
                    pe.wait_ge(s_init, 3)
                else:
                    pe.wait_ge(s_acc, 4 * (E + 1) + 1)
                clear_y((0, 1), True)
                gather(9 * p)
                with pe.Fori(0, E) as e:
                    u0 = moe_unit(p, e, 0)
                    j0 = E * STEPS * p + STEPS * e
                    idx = 9 * p + e
                    step(j0, 0, u0, True, False, idx + XT["gather"])
                    combine(idx, E * p + e)
                    turn_selection(E * p + e, e)
                    turn_hidden(j0, False)
                    pe.wait_ge(s_acc, 4 * (idx + 1) + 1)
                    clear_y((0, 1))
                    with pe.Fori(0, STEPS // 2 - 1) as i:
                        for d in range(2):
                            f = plus(u0, 4 + 6 * d)
                            step(j0 + 2 * i + (1 + d), (1 + d) % 2, (f[0] + 2 * i, f[1]), False, False)
                    for j in (STEPS - 2, STEPS - 1):
                        step(j0 + j, j % 2, plus(u0, 6 * j - 2), False, False, last=idx + 1 if j == STEPS - 1 else None)
                    wait_step(pe, m_htl, j0 + STEPS)
                    down(0, 0, plus(u0, PER_FFN - 2), False)
                    down(1, 0, plus(u0, PER_FFN - 1), False, True)
                combine(9 * p + E, E * (p + 1))

            experts(0)
            flag = pe.value_load(over_i[0:1, 0:1], min_val=0, max_val=1)
            with pe.If(flag > 0):
                experts(1)


def layout(v):
    def stationary(w):
        k, n = w.shape
        return w.reshape(k // P, P, n // P, P).transpose(1, 2, 0, 3).reshape(P, -1, UNIT).transpose(1, 0, 2)

    def moving(w):
        k, n = w.shape
        return w.reshape(k // P, P, n // NT, NT).transpose(1, 2, 0, 3).reshape(P, -1, UNIT).transpose(1, 0, 2)

    def glu(w):
        a = w.reshape(NC, P, 2, NC, P).transpose(1, 3, 2, 0, 4)
        return a.reshape(P, NC, UNIT).transpose(1, 0, 2)

    def swiglu(gu, down):
        g, u, d = moving(gu[:, :F]), moving(gu[:, F:]), down.reshape(2 * STEPS, 2, P, D).transpose(0, 2, 1, 3).reshape(-1, P, UNIT)
        parts = []
        for j in range(STEPS):
            parts += [g[2 * j:2 * j + 2], u[2 * j:2 * j + 2]]
            if j:
                parts.append(d[2 * j - 2:2 * j])
        return parts + [d[2 * STEPS - 2:]]

    wq, wkv, wo = v["xa_wq"], v["xa_wkv"], v["xa_wo"]
    parts = [stationary(wkv[0][:, :D]), moving(wkv[0][:, D:]),
             v["pool_w"][0].reshape(4, 2, P, S).transpose(2, 0, 1, 3).reshape(1, P, UNIT),
             stationary(wq[0]), moving(wo[0])]
    parts += swiglu(v["ffn_w_gu"][0], v["ffn_w_down"][0])
    parts += [glu(v["conv_pw1_w"][0]), stationary(wkv[1][:, :D]), moving(wkv[1][:, D:]), moving(v["conv_pw2_w"][0]),
              stationary(wq[1]), moving(wo[1])]
    for e in range(E):
        parts += swiglu(v["moe_w_gu"][0, e], v["moe_w_down"][0, e])
    stream = np.empty((UNITS, P, UNIT), np.float32)
    at = 0
    for p in parts:
        stream[at:at + len(p)] = p
        at += len(p)

    def chan(a):
        return a.reshape(-1, P).T

    cols = np.concatenate(
        [chan(a) for a in (v["mem_norm_g"], v["mix_pre_g"][0], v["xa_pre_g"][0], v["ffn_pre_g"][0], v["mix_pre_g"][1],
                           v["xa_pre_g"][1], v["ffn_pre_g"][1], v["conv_pw1_b"][0], v["conv_dw_b"][0], v["conv_ln_g"][0],
                           v["conv_ln_b"][0], v["conv_dw_w"][0])]
        + [v["moe_router"][0].reshape(NC, P, E).transpose(1, 0, 2).reshape(P, NC * E)], axis=1)
    recip = np.concatenate([1.0 / np.minimum(np.arange(S) + 1, w) for w in WINDOWS]).astype(np.float32)
    rows = np.stack([recip, v["pool_b"][0].reshape(D), v["pool_scale"][0], v["mix_post_g"][0], v["xa_post_g"][0],
                     v["ffn_post_g"][0], v["conv_pw2_b"][0], v["mix_post_g"][1], v["xa_post_g"][1], v["ffn_post_g"][1]])
    return {"x": v["x"], "mem": v["mem"], "stream": stream, "cols": cols, "rows": rows}


def kernel(**inputs):
    import concourse.bacc as bacc
    from concourse.bass_utils import run_bass_kernel_spmd

    arrays = {n: np.ascontiguousarray(a) for n, a in layout({n: np.asarray(a) for n, a in inputs.items()}).items()}
    nc = bacc.Bacc("TRN2", target_bir_lowering=False, num_devices=1)
    ins = [nc.dram_tensor(n, a.shape, F32, kind="ExternalInput").ap() for n, a in arrays.items()]
    out = nc.dram_tensor("out", (1, S, D), F32, kind="ExternalOutput").ap()
    build(nc, *ins, out)
    return run_bass_kernel_spmd(nc, [arrays], core_ids=[0]).results[0]["out"]
```

```python
from contextlib import ExitStack

import numpy as np

import concourse.bass as bass
from concourse import mybir

F32 = mybir.dt.float32
F32R = mybir.dt.float32r
I32 = mybir.dt.int32
ALU = mybir.AluOpType
ACT = mybir.ActivationFunctionType
AX = mybir.AxisListType

P = 128
D = 1024
S = 256
F = 3584
E = 8
HEADS = 4
TAPS = 31
WINDOWS = (2, 4, 8, 16)
EPS = 1e-6
NB = S // P
NC = D // P
PE_CHUNKS = (6, 7)
DIAGS = 16
GROUPS = ((0, 1), (2, 3), (4, 5))
UNIT = 2048
RING = 6
SPLIT = 3
TAPS_PW1, TAPS_KV = 3, 6
SHARE_CONV = 768
SHARE = 1792
NT = 512
STEPS = F // NT
PER_STEP = 6
PER_FFN = STEPS * PER_STEP
SLOTS = 128
PAD = 16
CPAD = TAPS - 1
BIG = 3.0e38
SCALE = float(D // HEADS) ** -0.5
COMBINE_BANKS = (5, 6, 0, 1)

_at = 0
U = {}
for _name, _n in (("k0", 4), ("v0", 4), ("pool", 1), ("q0", 4), ("o0", 4), ("ffn", PER_FFN), ("pw1", 8), ("k1", 4),
                  ("v1", 4), ("pw2", 4), ("q1", 4), ("o1", 4), ("moe", E * PER_FFN)):
    U[_name] = _at
    _at += _n
UNITS = _at

COL = {}
_at = 0
for _name, _n in (("mem", NC), ("mix0", NC), ("xa0", NC), ("ffn0", NC), ("mix1", NC), ("xa1", NC), ("ffn1", NC),
                  ("pw1_b", 2 * NC), ("dw_b", NC), ("ln_g", NC), ("ln_b", NC), ("dw_w", TAPS * NC), ("router", NC * E)):
    COL[_name] = _at
    _at += _n
COLS = _at
ROWS = ("recip", "pool_b", "pool_scale", "mix_post0", "xa_post0", "ffn_post0", "pw2_b", "mix_post1", "xa_post1", "ffn_post1")
ROW_SLOTS = 3

STAT = {n: i for i, n in enumerate(("mem", "mix0", "post_mix0", "xa0", "post_xa0", "ffn0", "post_ffn0", "mix1",
                                    "post_mix1", "xa1", "post_xa1", "ffn1", "post_ffn1"))}
TURN = {n: i for i, n in enumerate(("mem", "mix0", "xa0", "ffn0", "mix1", "mem_again", "xa1", "ffn1"))}
XN = {n: i for i, n in enumerate(("mem", "mix0", "mix1"))}
XT = {n: i for i, n in enumerate(("mem", "pooled", "xa0", "o0", "ffn0", "mix1", "mem_again", "z", "xa1", "o1", "ffn1",
                                  "gather"))}
RES = {n: i for i, n in enumerate(("mix0", "xa0", "ffn0", "mix1", "xa1"))}
POST = {n: i for i, n in enumerate(("post_mix0", "post_xa0", "post_ffn0", "post_mix1", "post_xa1", "post_ffn1"))}


def unit(n):
    return n // RING, n % RING


def plus(u, k):
    return u[0] + (u[1] + k) // RING, (u[1] + k) % RING


def build(nc, x, mem, stream, cols, rows, out):
    with ExitStack() as ctx:
        def sb(name, shape, dt=F32):
            return ctx.enter_context(nc.sbuf_tensor(name, shape, dt))

        def sem(name):
            return ctx.enter_context(nc.semaphore(name))

        raw = sb("raw", [P, RING, UNIT])
        w_hi = sb("w_hi", [P, SPLIT, UNIT], F32R)
        w_lo = sb("w_lo", [P, SPLIT, UNIT], F32R)
        xt_hi = sb("xt_hi", [P, NC * S], F32R)
        xt_lo = sb("xt_lo", [P, NC * S], F32R)
        hn_hi = sb("hn_hi", [P, 2 * D], F32R)
        hn_lo = sb("hn_lo", [P, 2 * D], F32R)
        ys_hi = sb("ys_hi", [P, D], F32R)
        ys_lo = sb("ys_lo", [P, D], F32R)
        res = sb("res", [P, NB, D])
        buf_k = sb("buf_k", [P, NC, S])
        buf_v = sb("buf_v", [P, NB, D])
        buf_a = sb("buf_a", [P, NC * (S + CPAD)])
        buf_b = sb("buf_b", [P, NC * (S + PAD)])
        buf_c = sb("buf_c", [P, NC * (S + PAD)])
        row = sb("row", [P, ROW_SLOTS, D])
        col = sb("col", [P, COLS])
        ident = sb("ident", [P, P])
        ones = sb("ones", [P, P])
        upper = sb("upper", [P, P])
        iota = sb("iota", [P, SLOTS])
        rank = sb("rank", [P, E])
        zeros = sb("zeros", [P, P], F32R)
        eps = sb("eps", [P, 1])
        silu_at = sb("silu_at", [P, 1])
        stat = sb("stat", [P, 3, len(STAT), NB])
        soft = sb("soft", [P, 4, HEADS * NB])
        soft_scale = sb("soft_scale", [P, 2, NB])
        ln_row = sb("ln_row", [P, 2, S])
        sel = sb("sel", [P, SLOTS * NB], F32R)
        sel_t = sb("sel_t", [P, SLOTS * NB], F32R)
        route = sb("route", [P, 10, NB, E])
        rtmp = sb("rtmp", [P, 8, NB])
        place = sb("place", [P, E + 1, NB])
        place2 = sb("place2", [P, E + 1, NB])
        gate = sb("gate", [P, E + 1, NB])
        slot_gate = sb("slot_gate", [P, 1])
        over = sb("over", [P, 1])
        over_i = sb("over_i", [P, 1], I32)
        ps = ctx.enter_context(nc.psum_tensor("ps", [P, 8, NT], F32))

        landed = [sem(f"landed{i}") for i in range(RING)]
        s_hi = sem("s_hi")
        s_lo_v = sem("s_lo_v")
        s_lo_p = sem("s_lo_p")
        s_used = sem("s_used")
        s_in, s_col, s_mem, s_mem2 = sem("s_in"), sem("s_col"), sem("s_mem"), sem("s_mem2")
        s_row = [sem(f"s_row{i}") for i in range(ROW_SLOTS)]
        s_const, s_zero, s_init = sem("s_const"), sem("s_zero"), sem("s_init")
        s_sq, s_inv = sem("s_sq"), sem("s_inv")
        s_xn, s_turn = sem("s_xn"), sem("s_turn")
        s_xth, s_xtl = sem("s_xth"), sem("s_xtl")
        s_res, s_t = sem("s_res"), sem("s_t")
        s_f0, s_pad, s_win, s_pd, s_pb = (sem(n) for n in ("s_f0", "s_pad", "s_win", "s_pd", "s_pb"))
        s_kc, s_vc, s_qc = (sem(n) for n in ("s_kc", "s_vc", "s_qc"))
        s_sc, s_nm, s_ex, s_pn = (sem(n) for n in ("s_sc", "s_nm", "s_ex", "s_pn"))
        s_pt, s_pte, s_pto, s_ov = (sem(n) for n in ("s_pt", "s_pte", "s_pto", "s_ov"))
        s_silu, s_mul, s_ht, s_hth, s_htl = (sem(n) for n in ("s_silu", "s_mul", "s_ht", "s_hth", "s_htl"))
        m_silu, m_mul, m_ht, m_hth, m_htl = (sem(n) for n in ("m_silu", "m_mul", "m_ht", "m_hth", "m_htl"))
        m_steps = (m_silu, m_mul, m_ht, m_hth, m_htl)
        s_sg, s_u, s_cv, s_ln, s_mu, s_xc, s_vq, s_vs, s_ly, s_z, s_p2, s_diag, s_dused, s_cb = (
            sem(n) for n in ("s_sg", "s_u", "s_cv", "s_ln", "s_mu", "s_xc", "s_vq", "s_vs", "s_ly", "s_z", "s_p2", "s_diag", "s_dused", "s_cb"))

        s_hnh, s_hnl, s_rh, s_rl, s_lg, s_rt, s_e2, s_e2x, s_sel, s_pos, s_over = (
            sem(n) for n in ("s_hnh", "s_hnl", "s_rh", "s_rl", "s_lg", "s_rt", "s_e2", "s_e2x", "s_sel", "s_pos", "s_over"))
        s_g, s_gath, s_gtp, s_gt, s_gs, s_ysh, s_ysl, s_comb, s_acc = (
            sem(n) for n in ("s_g", "s_gath", "s_gtp", "s_gt", "s_gs", "s_ysh", "s_ysl", "s_comb", "s_acc"))
        s_tab, s_lt = sem("s_tab"), sem("s_lt")
        s_fin0, s_fin, s_out = sem("s_fin0"), sem("s_fin"), sem("s_out")

        block = ctx.enter_context(nc.Block())

        router_hi = ys_hi[:, 0:NC * E]
        router_lo = ys_lo[:, 0:NC * E]
        xth = xt_hi[:, :].rearrange("p (c t) -> p c t", c=NC)
        xtl = xt_lo[:, :].rearrange("p (c t) -> p c t", c=NC)
        tok_a = buf_a[:, 0:NB * D].rearrange("p (b d) -> p b d", b=NB)
        tok_b = buf_b[:, 0:NB * D].rearrange("p (b d) -> p b d", b=NB)
        tok_c = buf_c[:, 0:NB * D].rearrange("p (b d) -> p b d", b=NB)
        chan_a = buf_a[:, 0:NC * S].rearrange("p (c t) -> p c t", c=NC)
        chan_b = buf_b[:, 0:NC * S].rearrange("p (c t) -> p c t", c=NC)
        chan_c = buf_c[:, 0:NC * S].rearrange("p (c t) -> p c t", c=NC)
        pool_a, pool_b, pool_c = (b[:, 0:NC * (S + PAD)].rearrange("p (c t) -> p c t", c=NC) for b in (buf_a, buf_b, buf_c))
        conv_u = buf_a[:, :].rearrange("p (c t) -> p c t", c=NC)
        acc = buf_k[:, :, :].rearrange("p (b c) t -> p b (c t)", b=NB)
        norm_diag = ln_row[:, :, :].rearrange("p k (b t) -> p k b t", b=NB)
        diags = buf_c[:, 0:DIAGS * P].rearrange("p (i n) -> p i n", i=DIAGS)
        sg_glu = buf_v[:, 0, 0:2 * S].rearrange("p (i t) -> p i t", i=2)
        y_ps = ps[:, 0:4, :].rearrange("p (b n) c -> p b n c", b=NB)
        y_tok = ps[:, 0:4, :].rearrange("p (b n) c -> p b (n c)", b=NB)

        def pooled(c):
            return (pool_b, pool_c)[c // 2 % 2][:, c, PAD:PAD + S]

        def gain(name, c):
            return col[:, COL[name] + c:COL[name] + c + 1]

        def turned(bank0, c):
            return ps[:, bank0 + c // 2, (c % 2) * S:(c % 2) * S + S]

        def wait_used(eng, u, lag):
            q, r = u
            if isinstance(q, int) and RING * q + r - lag + 1 <= 0:
                return
            eng.wait_ge(s_used, RING * q + (r - lag + 1))

        def wait_step(eng, s, count):
            if s in m_steps:
                eng.wait_ge(s, count + 1)
            elif not (isinstance(count, int) and count == 0):
                eng.wait_ge(s, count)

        def wait_low(eng, u):
            q, r = u
            eng.wait_ge(s_lo_v, RING * q + (r + 1))
            eng.wait_ge(s_lo_p, RING * q + (r + 1))

        def share(u):
            q, r = u
            return SHARE_CONV if isinstance(q, int) and U["pw1"] + 1 <= RING * q + r < U["pw2"] + 1 else SHARE

        def split_hi(act, u):
            q, r = u
            act.wait_ge(landed[r], 16 * (q + 1))
            wait_used(act, u, SPLIT)
            nc.scalar.activation(w_hi[:, r % SPLIT, :], raw[:, r, :], ACT.Copy).then_inc(s_hi, 1)

        def split_lo(dve, u):
            q, r = u
            m = share(u)
            dve.wait_ge(s_hi, RING * q + (r + 1))
            nc.vector.tensor_tensor(w_lo[:, r % SPLIT, 0:m], raw[:, r, 0:m], w_hi[:, r % SPLIT, 0:m].bitcast(F32),
                                    ALU.subtract).then_inc(s_lo_v, 1)

        def load(sp, u, index):
            q, r = u
            if not (isinstance(q, int) and q == 0):
                sp.wait_ge(s_lo_v, RING * q + (r + 1 - RING))
                sp.wait_ge(s_lo_p, RING * q + (r + 1 - RING))
            sp.dma_start(raw[:, r, :], stream[bass.ds(index, 1), :, :].rearrange("a p n -> p (a n)")
                         ).then_inc(landed[r], 16)

        def three(out_ap, a_hi, a_lo, wa_hi, wa_lo, start, stop, weights_stay):
            pairs = ((a_hi, wa_hi), (a_lo, wa_hi), (a_hi, wa_lo))
            for i, (a, w) in enumerate(pairs):
                lhs, rhs = (w, a) if weights_stay else (a, w)
                mm = nc.tensor.matmul(out_ap, lhs, rhs, start=start and i == 0, stop=stop and i == 2)
            return mm

        moe = U["moe"]
        MOE0 = unit(moe)

        def moe_unit(p, e, k):
            q, r = MOE0[0], MOE0[1] + k
            return q + STEPS * (E * p) + STEPS * e + r // RING, r % RING

        @block.sync
        def _(sp):
            sp.dma_start(tok_b, mem[0].rearrange("(b p) d -> p b d", p=P)).then_inc(s_mem, 16)
            sp.dma_start(col[:, :], cols).then_inc(s_col, 16)
            for n in range(moe):
                if n == SPLIT:
                    sp.dma_start(res[:, :, :], x[0].rearrange("(b p) d -> p b d", p=P)).then_inc(s_in, 16)
                load(sp, unit(n), n)
                if n == U["pw1"] + RING - 1:
                    sp.wait_ge(s_turn, NC * (TURN["mix1"] + 1))
                    sp.dma_start(tok_c, mem[0].rearrange("(b p) d -> p b d", p=P)).then_inc(s_mem2, 16)

            def experts(p):
                with sp.Fori(0, E * STEPS) as i:
                    for k in range(RING):
                        q, r = plus(MOE0, k)
                        load(sp, (q + E * STEPS * p + i, r), i * RING + (moe + k))

            experts(0)
            sp.wait_ge(s_over, 1)
            flag = sp.value_load(over_i[0:1, 0:1], min_val=0, max_val=1)
            with sp.If(flag > 0):
                experts(1)
            sp.wait_ge(s_fin, NB)
            sp.dma_start(out[0].rearrange("(b p) d -> p b d", p=P), res[:, :, :]).then_inc(s_out, 16)
            sp.wait_ge(s_out, 16)

        @block.gpsimd
        def _(pool):
            def split_lo(u):
                q, r = u
                m = share(u)
                pool.wait_ge(s_hi, RING * q + (r + 1))
                nc.gpsimd.tensor_tensor(w_lo[:, r % SPLIT, m:], raw[:, r, m:], w_hi[:, r % SPLIT, m:].bitcast(F32),
                                        ALU.subtract).then_inc(s_lo_p, 1)

            def split_next(n):
                while unit_at[0] < n:
                    split_lo(unit(unit_at[0]))
                    unit_at[0] += 1

            unit_at = [0]

            def load_row(i):
                pool.dma_start(row[:, i % ROW_SLOTS, :], rows[i:i + 1, :].partition_broadcast(P)
                               ).then_inc(s_row[i % ROW_SLOTS], 16)

            nc.gpsimd.memset(eps[:, :], EPS).then_inc(s_const, 1)
            nc.gpsimd.memset(ident[:, :], 0.0).then_inc(s_zero, 1)
            nc.gpsimd.memset(ones[:, :], 1.0).then_inc(s_zero, 1)
            pool.wait_ge(s_zero, 2)
            nc.gpsimd.affine_select(out=ident[:, :], in_=ident[:, :], compare_op=ALU.not_equal, fill=1.0, base=0,
                                    pattern=[[-1, P]], channel_multiplier=1).then_inc(s_const, 1)
            for i in range(ROW_SLOTS):
                load_row(i)
            nc.gpsimd.affine_select(out=upper[:, :], in_=ones[:, :], compare_op=ALU.is_gt, fill=0.0, base=0,
                                    pattern=[[1, P]], channel_multiplier=-1).then_inc(s_const, 1)
            nc.gpsimd.iota(iota[:, :], [[1, SLOTS]], base=0, channel_multiplier=0,
                           allow_small_or_imprecise_dtypes=True).then_inc(s_const, 1)
            nc.gpsimd.iota(rank[:, :], [[-1, E]], base=E, channel_multiplier=0,
                           allow_small_or_imprecise_dtypes=True).then_inc(s_const, 1)
            split_next(U["pool"] + 3)
            pool.wait_ge(s_pd, NC)
            load_row(3)
            pool.wait_ge(s_pb, 2 * NB)
            load_row(4)
            load_row(5)
            pool.wait_ge(s_t, NB)
            load_row(6)
            split_next(U["ffn"] + 3)
            pool.wait_ge(s_t, 2 * NB)
            load_row(7)
            split_next(U["pw1"] + 3)
            pool.wait_ge(s_t, 3 * NB)
            load_row(8)
            split_next(U["q1"] + 3)
            pool.wait_ge(s_p2, NB)
            load_row(9)
            split_next(U["o1"] + 2)
            pool.wait_ge(s_sc, 2 * HEADS)
            nc.gpsimd.memset(acc, 0.0).then_inc(s_acc, 1)
            split_next(moe)

            def experts(p):
                with pool.Fori(0, E * STEPS) as i:
                    for k in range(RING):
                        q, r = plus(MOE0, k)
                        split_lo((q + E * STEPS * p + i, r))

            experts(0)
            pool.wait_ge(s_over, 1)
            flag = pool.value_load(over_i[0:1, 0:1], min_val=0, max_val=1)
            with pool.If(flag > 0):
                experts(1)

        @block.scalar
        def _(act):
            at = [0]

            def ahead(n):
                while at[0] < min(n, moe):
                    split_hi(act, unit(at[0]))
                    at[0] += 1

            def statistics(name, src, junk, updated=None, made=None, banks=False):
                i = STAT[name]
                for b in range(NB):
                    if updated is not None:
                        act.wait_ge(s_res, NB * RES[updated] + b + 1)
                    if made is not None:
                        act.wait_ge(made[0], made[1] * (b + 1))
                    if banks and b == 1:
                        act.wait_ge(s_t, NB * POST[name] + 1)
                    nc.scalar.activation(junk[:, b, :], src[:, b, :], ACT.Square,
                                         accum_out=stat[:, 0, i, b:b + 1]).then_inc(s_sq, 1)

            def chunks_out(turn, gain_name, bank0=4):
                for c in range(NC):
                    act.wait_ge(s_turn, NC * TURN[turn] + (c | 1) + 1)
                    nc.scalar.activation(xth[:, c, :], turned(bank0, c), ACT.Copy, scale=gain(gain_name, c)
                                         ).then_inc(s_xth, 1)

            def chan_result(dst, s_mine, n0, between=None):
                for c in range(NC):
                    if c == NC // 2 and between is not None:
                        between()
                    ahead(n0 + c // 2 + 1 + SPLIT)
                    act.wait_ge(s_used, n0 + c // 2 + 1)
                    nc.scalar.copy(dst[:, c, :], ps[:, 4 + c % 4, 0:S]).then_inc(s_mine, 1)

            def values_out(n0, before_last=None):
                for n in range(2):
                    ahead(n0 + 2 * n + 1 + SPLIT)
                    act.wait_ge(s_used, n0 + 2 * n + 2)
                    if n == 1 and before_last is not None:
                        before_last()
                    for b in range(NB):
                        nc.scalar.copy(buf_v[:, b, n * NT:n * NT + NT], y_ps[:, b, n, :]).then_inc(s_vc, 1)

            def attention(layer):
                n0 = U[f"q{layer}"]
                ahead(n0 + SPLIT)
                chunks_out(f"xa{layer}", f"xa{layer}")
                statistics(f"xa{layer}", res, tok_b, f"mix{layer}")
                chan_result(chan_a, s_qc, n0)
                ahead(n0 + 4 + SPLIT)
                for h in range(HEADS):
                    for b in range(NB):
                        i = h * NB + b
                        act.wait_ge(s_nm, HEADS * layer + h + 1)
                        nc.scalar.activation(chan_b[:, i, :], ps[:, 4 + h, b * S:b * S + S], ACT.Exp,
                                             bias=soft[:, 1, i:i + 1], scale=soft_scale[:, 0, b:b + 1],
                                             accum_out=soft[:, 2, i:i + 1]).then_inc(s_ex, 1)
                for h in range(0, HEADS, 2):
                    act.wait_ge(s_pt, HEADS * layer + h + 1)
                    nc.scalar.copy(buf_c[:, h * 2 * S:(h + 1) * 2 * S], ps[:, 4 + h, :]).then_inc(s_pte, 1)
                for c in range(NC):
                    act.wait_ge(s_ov, NC * layer + (c | 1) + 1)
                    nc.scalar.copy(xth[:, c, :], turned(4, c)).then_inc(s_xth, 1)
                ahead(U[f"o{layer}"] + 3 + SPLIT)
                act.wait_ge(s_used, U[f"o{layer}"] + 4)
                statistics(f"post_xa{layer}", y_tok, tok_b, banks=True)
                ahead(U[f"o{layer}"] + 4 + SPLIT)

            act.wait_ge(s_const, 1)
            act.wait_ge(s_mem, 16)
            statistics("mem", tok_b, tok_a)
            act.wait_ge(s_col, 16)
            ahead(1)
            chunks_out("mem", "mem")
            ahead(SPLIT)
            nc.scalar.copy(router_hi[:, :], col[:, COL["router"]:COL["router"] + NC * E]).then_inc(s_rh, 1)
            act.wait_ge(s_in, 16)
            statistics("mix0", res, tok_c)

            def mixer_input():
                for c in range(NC):
                    act.wait_ge(s_turn, NC * TURN["mix0"] + (c | 1) + 1)
                    nc.scalar.activation(pool_a[:, c, PAD:PAD + S], turned(0, c), ACT.Copy, scale=gain("mix0", c)
                                         ).then_inc(s_f0, 1)

            def pooled_high():
                for c in range(NC):
                    act.wait_ge(s_pd, c + 1)
                    nc.scalar.copy(xth[:, c, :], pooled(c)).then_inc(s_xth, 1)

            chan_result(buf_k, s_kc, U["k0"], mixer_input)
            values_out(U["v0"], pooled_high)
            ahead(U["pool"] + 1 + SPLIT)
            statistics("post_mix0", tok_b, tok_a, made=(s_pb, 2))
            attention(0)

            ahead(U["ffn"] + SPLIT)
            chunks_out("ffn0", "ffn0", 0)
            statistics("ffn0", res, tok_b, "xa0")
            act.wait_ge(s_inv, STAT["ffn0"] + 1)

            def hidden_silu(j, s_silu_, s_ht_, nb, bank, u_gate):
                wait_used(act, u_gate, -1)
                wait_step(act, s_ht_, j)
                if nb == 1:
                    nc.scalar.activation(buf_c[:, 0:NT], ps[:, bank, :], ACT.Silu).then_inc(s_silu_, 1)
                    return
                for b in range(nb):
                    ins = nc.scalar.activation(buf_c[:, b * NT:(b + 1) * NT], ps[:, bank + b, :], ACT.Silu,
                                               scale=stat[:, 2, STAT["ffn0"], b:b + 1])
                ins.then_inc(s_silu_, 1)

            def hidden_hi(j, par, s_ht_, s_hth_, dst, src):
                wait_step(act, s_ht_, j + 1)
                nc.scalar.copy(dst, src).then_inc(s_hth_, 1)

            def step(j, par, u0, first, dense, before=None, last=None):
                if dense:
                    sems, nb, bank = (s_silu, s_ht, s_hth), NB, 4
                    dst, src = hn_hi[:, par * 1024:par * 1024 + 1024], ps[:, 4:6, :].rearrange("p b n -> p (b n)")
                else:
                    sems, nb, bank = (m_silu, m_ht, m_hth), 1, 2
                    dst, src = xt_hi[:, 1024 + par * NT:1024 + par * NT + NT], ps[:, 4, :]
                if first:
                    split_hi(act, plus(u0, 3))
                    if before is not None:
                        gated(before)
                    split_hi(act, plus(u0, 4))
                    hidden_silu(j, sems[0], sems[1], nb, bank, u0)
                    split_hi(act, plus(u0, 5))
                    return (j, par, sems[1], sems[2], dst, src)
                for k in (2, 3, 4):
                    split_hi(act, plus(u0, k))
                hidden_silu(j, sems[0], sems[1], nb, bank, u0)
                split_hi(act, plus(u0, 5))
                if last is not None:
                    gathered(last)
                split_hi(act, plus(u0, 6))
                hidden_hi(j, par, sems[1], sems[2], dst, src)
                split_hi(act, plus(u0, 7))

            u0 = unit(U["ffn"])
            hidden_hi(*step(0, 0, u0, True, True))
            with act.Fori(0, STEPS // 2) as i:
                for d in range(2):
                    f = plus(u0, 4 + 6 * d)
                    step(2 * i + (1 + d), (1 + d) % 2, (f[0] + 2 * i, f[1]), False, True)
            at[0] = U["pw1"]
            ahead(U["pw1"] - 1 + SPLIT)
            act.wait_ge(s_used, U["pw1"])
            statistics("post_ffn0", y_tok, tok_b, banks=True)
            ahead(U["pw1"] + SPLIT)

            statistics("mix1", res, tok_b, "ffn0")
            chunks_out("mix1", "mix1")
            for c in range(NC):
                ahead(U["pw1"] + c + 1 + SPLIT)
                act.wait_ge(s_used, U["pw1"] + c + 1)
                if c >= 2:
                    act.wait_ge(s_u, c - 1)
                nc.scalar.activation(sg_glu[:, c % 2, :], ps[:, 5 + 2 * (c % 2), 0:S], ACT.Sigmoid,
                                     bias=gain("pw1_b", NC + c)).then_inc(s_sg, 1)
            chunks_out("mem_again", "mem", 0)

            def diagonals(i0, i1):
                for i in range(i0, i1):
                    if i >= DIAGS:
                        act.wait_ge(s_dused, i - DIAGS + 1)
                    nc.scalar.activation(diags[:, i % DIAGS, :], ident[:, :], ACT.Copy, scale=gain("dw_w", i % TAPS * NC + PE_CHUNKS[i // TAPS])
                                         ).then_inc(s_diag, 1)

            diagonals(0, DIAGS)
            chan_result(buf_k, s_kc, U["k1"])
            act.wait_ge(s_u, NC)
            values_out(U["v1"])
            ahead(U["pw2"] + SPLIT)
            diagonals(DIAGS, TAPS * len(PE_CHUNKS))
            for n, c in enumerate(PE_CHUNKS):
                act.wait_ge(s_dused, TAPS * (n + 1))
                nc.scalar.activation(chan_b[:, c, :], ps[:, 6 + n, 0:S], ACT.Identity, bias=gain("dw_b", c)).then_inc(s_cb, 1)
            for c in range(NC):
                act.wait_ge(s_xc, c + 1)
                nc.scalar.activation(chan_c[:, c, :], chan_b[:, c, :], ACT.Square).then_inc(s_vq, 1)
            act.wait_ge(s_ln, 2)
            nc.scalar.activation(ln_row[:, 1, :], ps[:, 5, 0:S], ACT.Sqrt, scale=1.0 / D, bias=eps[:, 0:1]).then_inc(s_vs, 1)
            for c in range(NC):
                act.wait_ge(s_ly, c + 1)
                nc.scalar.activation(chan_c[:, c, :], chan_b[:, c, :], ACT.Silu, scale=gain("ln_g", c), bias=gain("ln_b", c)
                                     ).then_inc(s_z, 1)
                nc.scalar.activation(xth[:, c, :], chan_b[:, c, :], ACT.Silu, scale=gain("ln_g", c), bias=gain("ln_b", c)
                                     ).then_inc(s_xth, 1)
            ahead(U["pw2"] + 3 + SPLIT)
            statistics("post_mix1", tok_a, tok_c, made=(s_p2, 1))
            ahead(U["pw2"] + 4 + SPLIT)
            attention(1)

            chunks_out("ffn1", "ffn1")
            statistics("ffn1", res, tok_b, "xa1")
            act.wait_ge(s_inv, STAT["ffn1"] + 1)
            for b in range(NB):
                nc.scalar.activation(hn_hi[:, b * D:b * D + D], res[:, b, :], ACT.Copy, scale=stat[:, 2, STAT["ffn1"], b:b + 1]
                                     ).then_inc(s_hnh, 1)
            for k in range(SPLIT):
                split_hi(act, unit(moe + k))
            act.wait_ge(s_e2, 1)
            nc.scalar.activation(rtmp[:, 5, :], rtmp[:, 4, :], ACT.Exp).then_inc(s_e2x, 1)

            def gathered(idx):
                for c in range(NC):
                    act.wait_ge(s_gath, 2 * idx + c // 4 + 1)
                    nc.scalar.activation(xt_hi[:, c * P:c * P + P], ps[:, 5 + c // 4, (c % 4) * P:(c % 4) * P + P], ACT.Copy,
                                         scale=gain("ffn1", c)).then_inc(s_xth, 1)

            def gated(idx):
                for n in range(2):
                    nc.scalar.activation(ys_hi[:, n * NT:n * NT + NT], ps[:, n, :], ACT.Copy, scale=slot_gate[:, 0:1]
                                         ).then_inc(s_ysh, 1)

            def experts(p):
                nc.scalar.activation(silu_at[:, :], eps[:, :], ACT.Silu).then_inc(s_tab, 1)
                gathered(9 * p)

                def expert(e, first):
                    u0 = moe_unit(p, e, 0)
                    j0 = E * STEPS * p + STEPS * e
                    if not (first and p == 0):
                        for k in range(SPLIT):
                            split_hi(act, plus(u0, k))
                    if not first:
                        wait_used(act, u0, 1)
                        act.wait_ge(s_gs, E * p + e)
                    late = step(j0, 0, u0, True, False, before=None if first else E * p + e - 1)
                    act.wait_ge(s_gtp, E * p + e + 1)
                    nc.scalar.copy(sel_t[:, :], ps[:, 7, 0:NB * SLOTS]).then_inc(s_gt, 1)
                    hidden_hi(*late)
                    with act.Fori(0, STEPS // 2 - 1) as i:
                        for d in range(2):
                            f = plus(u0, 4 + 6 * d)
                            step(j0 + 2 * i + (1 + d), (1 + d) % 2, (f[0] + 2 * i, f[1]), False, False)
                    for j in (STEPS - 2, STEPS - 1):
                        step(j0 + j, j % 2, plus(u0, 6 * j - 2), False, False, last=9 * p + e + 1 if j == STEPS - 1 else None)

                expert(0, True)
                with act.Fori(1, E) as e:
                    expert(e, False)
                wait_used(act, moe_unit(p, E, 0), 1)
                act.wait_ge(s_gs, E * (p + 1))
                gated(E * p + E - 1)

            experts(0)
            act.wait_ge(s_over, 1)
            flag = act.value_load(over_i[0:1, 0:1], min_val=0, max_val=1)
            with act.If(flag > 0):
                experts(1)
            act.wait_ge(s_fin0, 1)
            statistics("post_ffn1", acc, tok_b)

        @block.vector
        def _(dve):
            at = [0]
            chain = [0]

            def ahead(n):
                while at[0] < min(n, moe):
                    split_lo(dve, unit(at[0]))
                    at[0] += 1

            def link(ins):
                chain[0] += 1
                ins.then_inc(s_rt, 1)
                dve.wait_ge(s_rt, chain[0])

            def root_inverse(name):
                i = STAT[name]
                dve.wait_ge(s_sq, NB * (i + 1))
                mean, half, y = (stat[:, k, i, :] for k in range(3))
                link(nc.vector.tensor_scalar(mean, mean, 1.0 / D, EPS, ALU.mult, ALU.add))
                link(nc.vector.tensor_scalar(half.bitcast(I32), mean.bitcast(I32), 1, None, ALU.logical_shift_right))
                link(nc.vector.tensor_scalar(y.bitcast(I32), half.bitcast(I32), -1.0, float(0x5F3759DF), ALU.mult, ALU.add))
                for n in range(3):
                    link(nc.vector.scalar_tensor_tensor(out=half, in0=y, scalar=-0.5, in1=y, op0=ALU.mult, op1=ALU.mult))
                    link(nc.vector.tensor_tensor(half, half, mean, ALU.mult))
                    ins = nc.vector.scalar_tensor_tensor(out=y, in0=half, scalar=1.5, in1=y, op0=ALU.add, op1=ALU.mult)
                    if n < 2:
                        link(ins)
                ins.then_inc(s_inv, 1)
                dve.wait_ge(s_inv, i + 1)

            def norm_diagonal(name, k):
                for b in range(NB):
                    nc.vector.tensor_scalar(norm_diag[:, k, b, :], ident[:, :], stat[:, 2, STAT[name], b:b + 1], None, ALU.mult
                                            ).then_inc(s_xn, 1)

            def chunks_rest(xt, gain_name, bank0=4):
                for c in range(NC):
                    dve.wait_ge(s_xth, NC * XT[xt] + (c | 1) + 1)
                    nc.vector.scalar_tensor_tensor(out=xtl[:, c, :], in0=turned(bank0, c), scalar=gain(gain_name, c),
                                                   in1=xth[:, c, :].bitcast(F32), op0=ALU.mult, op1=ALU.subtract
                                                   ).then_inc(s_xtl, 1)

            def add_to_residual(name, src, row_index, t, done=None):
                i = STAT[name]
                k = POST[name]
                dve.wait_ge(s_row[row_index % ROW_SLOTS], 16 * (row_index // ROW_SLOTS + 1))
                for b in (1, 0):
                    if b == 0:
                        dve.wait_ge(s_sq, NB * i + 1)
                    nc.vector.tensor_tensor(t[:, b, :], src[:, b, :], row[:, row_index % ROW_SLOTS, :], ALU.mult
                                            ).then_inc(s_t, 1)
                root_inverse(name)
                dve.wait_ge(s_t, NB * k + NB)
                for b in range(NB):
                    nc.vector.scalar_tensor_tensor(out=res[:, b, :], in0=t[:, b, :], scalar=stat[:, 2, i, b:b + 1],
                                                   in1=res[:, b, :], op0=ALU.mult, op1=ALU.add).then_inc(done or s_res, 1)

            def attention(layer):
                n0 = U[f"q{layer}"]
                ahead(n0 + SPLIT)
                chunks_rest(f"xa{layer}", f"xa{layer}")
                root_inverse(f"xa{layer}")
                norm = stat[:, 2, STAT[f"xa{layer}"], :]
                link(nc.vector.tensor_scalar(soft_scale[:, 0, :], norm, SCALE, None, ALU.mult))
                link(nc.vector.tensor_scalar(soft_scale[:, 1, :], norm, -SCALE, None, ALU.mult))
                ahead(n0 + 4 + SPLIT)

                def maximum(h):
                    i = slice(h * NB, (h + 1) * NB)
                    dve.wait_ge(s_sc, HEADS * layer + h + 1)
                    link(nc.vector.tensor_reduce(soft[:, 0, i], ps[:, 4 + h, :].rearrange("p (b m) -> p b m", b=NB), AX.X,
                                                 ALU.max))
                    nc.vector.tensor_tensor(soft[:, 1, i], soft[:, 0, i], soft_scale[:, 1, :], ALU.mult).then_inc(s_nm, 1)

                def probabilities(h):
                    dve.wait_ge(s_ex, NC * layer + NB * (h + 1))
                    link(nc.vector.reciprocal(soft[:, 3, h * NB:(h + 1) * NB], soft[:, 2, h * NB:(h + 1) * NB]))
                    for i in range(h * NB, (h + 1) * NB):
                        nc.vector.tensor_scalar(chan_b[:, i, :], chan_b[:, i, :], soft[:, 3, i:i + 1], None, ALU.mult
                                                ).then_inc(s_pn, 1)

                maximum(0)
                for h in range(1, HEADS):
                    maximum(h)
                    probabilities(h - 1)
                probabilities(HEADS - 1)
                for h in range(1, HEADS, 2):
                    dve.wait_ge(s_pt, HEADS * layer + h + 1)
                    nc.vector.tensor_copy(buf_c[:, h * 2 * S:(h + 1) * 2 * S], ps[:, 4 + h, :]).then_inc(s_pto, 1)
                for c in range(NC):
                    dve.wait_ge(s_xth, NC * XT[f"o{layer}"] + (c | 1) + 1)
                    nc.vector.tensor_tensor(xtl[:, c, :], turned(4, c), xth[:, c, :].bitcast(F32), ALU.subtract
                                            ).then_inc(s_xtl, 1)
                ahead(U[f"o{layer}"] + 3 + SPLIT)
                dve.wait_ge(s_used, U[f"o{layer}"] + 4)
                add_to_residual(f"post_xa{layer}", y_tok, 4 + 4 * layer, tok_c)
                ahead(U[f"o{layer}"] + 4 + SPLIT)

            nc.vector.memset(zeros[:, :].bitcast(F32), 0.0).then_inc(s_init, 1)
            for s in m_steps:
                dve.sem_inc(s, 1)
            nc.vector.memset(place[:, :, :], -1.0).then_inc(s_init, 1)
            nc.vector.memset(gate[:, :, :], 0.0).then_inc(s_init, 1)
            root_inverse("mem")
            dve.wait_ge(s_const, 2)
            norm_diagonal("mem", 1)
            dve.wait_ge(s_col, 16)
            ahead(1)
            chunks_rest("mem", "mem")
            ahead(SPLIT)
            root_inverse("mix0")
            norm_diagonal("mix0", 0)
            dve.wait_ge(s_rh, 1)
            nc.vector.tensor_tensor(router_lo[:, :], col[:, COL["router"]:COL["router"] + NC * E], router_hi[:, :].bitcast(F32),
                                    ALU.subtract).then_inc(s_rl, 1)
            dve.wait_ge(s_turn, NC)
            nc.vector.memset(pool_a[:, :, 0:PAD], 0.0).then_inc(s_pad, 1)
            ahead(U["k0"] + 5)
            dve.wait_ge(s_f0, NC)
            dve.wait_ge(s_turn, 2 * NC)
            dve.wait_ge(s_pad, 1)
            src, lead = pool_a, 0
            for g, w in enumerate(WINDOWS):
                c0, lead = 2 * g, lead + w // 2
                dst = (pool_b, pool_c)[g % 2]
                nc.vector.tensor_tensor(dst[:, c0:NC, lead:], src[:, c0:NC, lead:], src[:, c0:NC, lead - w // 2:PAD + S - w // 2],
                                        ALU.add).then_inc(s_win, 1)
                dve.wait_ge(s_win, g + 1)
                src = dst
            dve.wait_ge(s_row[0], 16)
            for c in range(NC):
                p_c = pooled(c)
                nc.vector.tensor_tensor(p_c, p_c, row[:, 0, (c // 2) * S:(c // 2 + 1) * S], ALU.mult).then_inc(s_win, 1)
            for c in range(NC):
                p_c = pooled(c)
                dve.wait_ge(s_win, len(WINDOWS) + c + 1)
                nc.vector.tensor_tensor(p_c, p_c, pool_a[:, c, PAD:PAD + S], ALU.subtract).then_inc(s_pd, 1)
            ahead(U["pool"] + 2)
            for c in range(NC):
                dve.wait_ge(s_xth, NC * XT["pooled"] + c + 1)
                nc.vector.tensor_tensor(xtl[:, c, :], pooled(c), xth[:, c, :].bitcast(F32), ALU.subtract
                                        ).then_inc(s_xtl, 1)
            ahead(U["pool"] + SPLIT)
            dve.wait_ge(s_used, U["pool"] + 1)
            for r in (1, 2):
                dve.wait_ge(s_row[r], 16)
            for b in range(NB):
                nc.vector.tensor_tensor(tok_b[:, b, :], y_tok[:, b, :], row[:, 1, :], ALU.add).then_inc(s_pb, 1)
                dve.wait_ge(s_pb, 2 * b + 1)
                nc.vector.tensor_tensor(tok_b[:, b, :], tok_b[:, b, :], row[:, 2, :], ALU.mult).then_inc(s_pb, 1)
            dve.wait_ge(s_pb, 2 * NB)
            add_to_residual("post_mix0", tok_b, 3, tok_c)
            ahead(U["pool"] + 1 + SPLIT)
            attention(0)

            ahead(U["ffn"] + SPLIT)
            chunks_rest("ffn0", "ffn0", 0)
            root_inverse("ffn0")

            def hidden_mul(j, s_silu_, s_mul_, nb, bank, u_up):
                wait_step(dve, s_silu_, j + 1)
                wait_used(dve, u_up, -1)
                if nb == 1:
                    nc.vector.tensor_tensor(buf_c[:, 0:NT], buf_c[:, 0:NT], ps[:, bank, :], ALU.mult).then_inc(s_mul_, 1)
                    return
                for b in range(nb):
                    h = buf_c[:, b * NT:(b + 1) * NT]
                    ins = nc.vector.scalar_tensor_tensor(out=h, in0=ps[:, bank + b, :], scalar=stat[:, 2, STAT["ffn0"], b:b + 1],
                                                         in1=h, op0=ALU.mult, op1=ALU.mult)
                ins.then_inc(s_mul_, 1)

            def hidden_lo(j, s_hth_, s_htl_, dst, src, high):
                wait_step(dve, s_hth_, j + 1)
                nc.vector.tensor_tensor(dst, src, high.bitcast(F32), ALU.subtract).then_inc(s_htl_, 1)

            def step(j, par, u0, first, dense, before=None, last=None):
                if dense:
                    sems, nb, bank = (s_silu, s_mul, s_hth, s_htl), NB, 6
                    a, n = par * 1024, 1024
                    dst, high, src = hn_lo[:, a:a + n], hn_hi[:, a:a + n], ps[:, 4:6, :].rearrange("p b n -> p (b n)")
                else:
                    sems, nb, bank = (m_silu, m_mul, m_hth, m_htl), 1, 3
                    a, n = 1024 + par * NT, NT
                    dst, high, src = xt_lo[:, a:a + n], xt_hi[:, a:a + n], ps[:, 4, :]
                late = (j, sems[2], sems[3], dst, src, high)
                if first:
                    split_lo(dve, plus(u0, 3))
                    if before is not None:
                        gated(*before)
                    split_lo(dve, plus(u0, 4))
                    hidden_mul(j, sems[0], sems[1], nb, bank, plus(u0, 2))
                    split_lo(dve, plus(u0, 5))
                    return late
                for k in (2, 3, 4, 5):
                    split_lo(dve, plus(u0, k))
                hidden_mul(j, sems[0], sems[1], nb, bank, plus(u0, 2))
                if last is not None:
                    gathered(last)
                split_lo(dve, plus(u0, 6))
                hidden_lo(*late)
                split_lo(dve, plus(u0, 7))

            u0 = unit(U["ffn"])
            hidden_lo(*step(0, 0, u0, True, True))
            with dve.Fori(0, STEPS // 2) as i:
                for d in range(2):
                    f = plus(u0, 4 + 6 * d)
                    step(2 * i + (1 + d), (1 + d) % 2, (f[0] + 2 * i, f[1]), False, True)
            at[0] = U["pw1"]
            ahead(U["pw1"] - 1 + SPLIT)
            dve.wait_ge(s_used, U["pw1"])
            add_to_residual("post_ffn0", y_tok, 5, tok_c)

            root_inverse("mix1")
            norm_diagonal("mix1", 0)
            ahead(U["pw1"] + SPLIT)
            chunks_rest("mix1", "mix1")
            nc.vector.memset(conv_u[:, :, 0:CPAD], 0.0).then_inc(s_pad, 1)

            def gated_unit(c):
                dve.wait_ge(s_sg, c + 1)
                nc.vector.scalar_tensor_tensor(out=conv_u[:, c, CPAD:], in0=ps[:, 4 + 2 * (c % 2), 0:S], scalar=gain("pw1_b", c),
                                               in1=sg_glu[:, c % 2, :], op0=ALU.add, op1=ALU.mult).then_inc(s_u, 1)

            tap_at = [0, 0, 0]

            def taps(n):
                for _ in range(n):
                    g, j, done = tap_at
                    if g == len(GROUPS):
                        return
                    group = GROUPS[g]
                    dve.wait_ge(s_u, group[-1] + 1)
                    for i in group:
                        k = COL["dw_w"] + j * NC + i
                        w, v, u = col[:, k:k + 1], chan_b[:, i, :], conv_u[:, i, j:j + S]
                        if j == 0:
                            ins = nc.vector.tensor_scalar(v, u, w, gain("dw_b", i), ALU.mult, ALU.add)
                        else:
                            dve.wait_ge(s_cv, done - len(group) + 1)
                            ins = nc.vector.scalar_tensor_tensor(out=v, in0=u, scalar=w, in1=v, op0=ALU.mult, op1=ALU.add)
                        ins.then_inc(s_cv, 1)
                        done += 1
                    tap_at[:] = (g, j + 1, done) if j + 1 < TAPS else (g + 1, 0, done)

            dve.wait_ge(s_pad, 2)
            for c in range(NC):
                ahead(U["pw1"] + c + 1 + SPLIT)
                gated_unit(c)
                if c >= 2:
                    taps(TAPS_PW1)
            chunks_rest("mem_again", "mem", 0)
            for n in range(U["k1"] + SPLIT, U["pw2"]):
                taps(TAPS_KV)
                ahead(n + 1)
            taps(TAPS * len(GROUPS))
            ahead(U["pw2"] + SPLIT)
            dve.wait_ge(s_ln, 1)
            nc.vector.tensor_scalar(ln_row[:, 0, :], ps[:, 4, 0:S], -1.0 / D, None, ALU.mult).then_inc(s_mu, 1)
            dve.wait_ge(s_mu, 1)
            dve.wait_ge(s_cv, TAPS * sum(len(g) for g in GROUPS))
            dve.wait_ge(s_cb, len(PE_CHUNKS))
            for c in range(NC):
                nc.vector.tensor_tensor(chan_b[:, c, :], chan_b[:, c, :], ln_row[:, 0, :], ALU.add).then_inc(s_xc, 1)
            dve.wait_ge(s_vs, 1)
            nc.vector.reciprocal(ln_row[:, 0, :], ln_row[:, 1, :]).then_inc(s_mu, 1)
            dve.wait_ge(s_mu, 2)
            for c in range(NC):
                dve.wait_ge(s_xc, c + 1)
                nc.vector.tensor_tensor(chan_b[:, c, :], chan_b[:, c, :], ln_row[:, 0, :], ALU.mult).then_inc(s_ly, 1)
            for c in range(NC):
                dve.wait_ge(s_xth, NC * XT["z"] + c + 1)
                nc.vector.tensor_tensor(xtl[:, c, :], chan_c[:, c, :], xth[:, c, :].bitcast(F32), ALU.subtract).then_inc(s_xtl, 1)
            ahead(U["pw2"] + 3 + SPLIT)
            dve.wait_ge(s_used, U["pw2"] + 4)
            dve.wait_ge(s_row[0], 48)
            for b in range(NB):
                nc.vector.tensor_tensor(tok_a[:, b, :], y_tok[:, b, :], row[:, 0, :], ALU.add).then_inc(s_p2, 1)
            dve.wait_ge(s_p2, NB)
            add_to_residual("post_mix1", tok_a, 7, tok_b)
            ahead(U["pw2"] + 4 + SPLIT)
            attention(1)
            chunks_rest("ffn1", "ffn1")
            root_inverse("ffn1")
            norm = stat[:, 2, STAT["ffn1"], :]

            def normalised_lo(b):
                dve.wait_ge(s_hnh, b + 1)
                h = slice(b * D, b * D + D)
                nc.vector.scalar_tensor_tensor(out=hn_lo[:, h], in0=res[:, b, :], scalar=norm[:, b:b + 1],
                                               in1=hn_hi[:, h].bitcast(F32), op0=ALU.mult, op1=ALU.subtract).then_inc(s_hnl, 1)

            normalised_lo(0)
            lg, eq, key1, key2, rest, g1, g2, chosen = (route[:, i, :, :] for i in range(8))
            top1, best, top2, best2, diff, expd, w1, w2 = (rtmp[:, i, :] for i in range(8))
            ranks = rank[:, None, :].broadcast_to([P, NB, E])

            def wide(a):
                return a[:, :, None].broadcast_to([P, NB, E])

            dve.wait_ge(s_const, 5)
            dve.wait_ge(s_init, 3)
            dve.wait_ge(s_lg, 1)
            nc.vector.tensor_copy(ln_row[0:E, 0, :], ps[0:E, 2, 0:S]).then_inc(s_lt, 1)
            dve.wait_ge(s_lg, 2)
            for b in range(NB):
                link(nc.vector.tensor_scalar(lg[:, b, :], ps[:, 1, b * E:(b + 1) * E], norm[:, b:b + 1], None, ALU.mult))
            for vals, top, b_, key in ((lg, top1, best, key1), (rest, top2, best2, key2)):
                link(nc.vector.tensor_reduce(top, vals, AX.X, ALU.max))
                link(nc.vector.tensor_tensor(eq, vals, wide(top), ALU.is_equal))
                link(nc.vector.tensor_tensor(eq, eq, ranks, ALU.mult))
                link(nc.vector.tensor_reduce(b_, eq, AX.X, ALU.max))
                link(nc.vector.tensor_tensor(key, eq, wide(b_), ALU.is_equal))
                if vals is lg:
                    link(nc.vector.scalar_tensor_tensor(out=rest, in0=key1, scalar=-BIG, in1=lg, op0=ALU.mult, op1=ALU.add))
            nc.vector.tensor_tensor(chosen, key1, key2, ALU.add).then_inc(s_sel, 1)
            nc.vector.tensor_tensor(diff, top2, top1, ALU.subtract).then_inc(s_e2, 1)
            normalised_lo(1)
            dve.wait_ge(s_pos, 1)
            dve.wait_ge(s_sel, 1)
            link(nc.vector.scalar_tensor_tensor(out=g2, in0=ps[:, 0, 64:64 + NB * E].rearrange("p (b e) -> p b e", b=NB), scalar=1.0,
                                                in1=chosen, op0=ALU.add, op1=ALU.mult))
            link(nc.vector.tensor_scalar(place[:, 0:E, :].rearrange("p e b -> p b e"), g2, -1.0, None, ALU.add))

            def select(where, e):
                for b in range(NB):
                    nc.vector.tensor_scalar(sel[:, b * SLOTS:(b + 1) * SLOTS], iota[:, :],
                                            where[:, bass.ds(e, 1), b], None, ALU.is_equal).then_inc(s_g, 1)

            def gathered(idx):
                for c in range(NC):
                    dve.wait_ge(s_xth, NC * (XT["gather"] + idx) + ((c | 3) + 1))
                    o = slice(c * P, c * P + P)
                    nc.vector.scalar_tensor_tensor(out=xt_lo[:, o], in0=ps[:, 5 + c // 4, (c % 4) * P:(c % 4) * P + P],
                                                   scalar=gain("ffn1", c), in1=xt_hi[:, o].bitcast(F32), op0=ALU.mult,
                                                   op1=ALU.subtract).then_inc(s_xtl, 1)

            def gated(idx, count):
                dve.wait_ge(s_gs, count)
                for n in range(2):
                    dve.wait_ge(s_ysh, 2 * idx + n + 1)
                    o = slice(n * NT, n * NT + NT)
                    nc.vector.scalar_tensor_tensor(out=ys_lo[:, o], in0=ps[:, n, :], scalar=slot_gate[:, 0:1],
                                                   in1=ys_hi[:, o].bitcast(F32), op0=ALU.mult, op1=ALU.subtract
                                                   ).then_inc(s_ysl, 1)

            def combined(idx):
                dve.wait_ge(s_acc, 4 * idx + 1)
                for i, bank in enumerate(COMBINE_BANKS):
                    dve.wait_ge(s_comb, 4 * idx + i + 1)
                    a = acc[:, i // 2, (i % 2) * NT:(i % 2) * NT + NT]
                    nc.vector.tensor_tensor(a, a, ps[:, bank, :], ALU.add).then_inc(s_acc, 1)

            def gates():
                dve.wait_ge(s_e2x, 1)
                link(nc.vector.tensor_scalar(w2, expd, 1.0, None, ALU.add))
                link(nc.vector.reciprocal(w1, w2))
                link(nc.vector.tensor_tensor(w2, expd, w1, ALU.mult))
                link(nc.vector.tensor_tensor(g1, key1, wide(w1), ALU.mult))
                link(nc.vector.tensor_tensor(g2, key2, wide(w2), ALU.mult))
                link(nc.vector.tensor_tensor(gate[:, 0:E, :].rearrange("p e b -> p b e"), g1, g2, ALU.add))
                link(nc.vector.tensor_scalar(place2[:, :, :], place[:, :, :], -float(SLOTS), None, ALU.add))
                link(nc.vector.tensor_reduce(over[:, :], ps[:, 0, 128:128 + E], AX.X, ALU.max))
                nc.vector.tensor_scalar(over_i[:, :], over[:, :], float(SLOTS) + 0.5, None, ALU.is_gt).then_inc(s_over, 1)

            def experts(p):
                where = (place, place2)[p]
                select(where, 0)
                if p == 0:
                    for k in range(SPLIT):
                        split_lo(dve, unit(moe + k))
                    gates()
                gathered(9 * p)

                def expert(e, first):
                    u0 = moe_unit(p, e, 0)
                    j0 = E * STEPS * p + STEPS * e
                    if not (first and p == 0):
                        for k in range(SPLIT):
                            split_lo(dve, plus(u0, k))
                    late = step(j0, 0, u0, True, False, before=None if first else (E * p + e - 1, E * p + e))
                    if not first:
                        combined(E * p + e - 1)
                    dve.wait_ge(s_gt, E * p + e + 1)
                    nc.vector.tensor_copy(slot_gate[:, :], ps[:, 7, 2 * SLOTS:2 * SLOTS + 1]).then_inc(s_gs, 1)
                    hidden_lo(*late)
                    select(where, e + 1)
                    with dve.Fori(0, STEPS // 2 - 1) as i:
                        for d in range(2):
                            f = plus(u0, 4 + 6 * d)
                            step(j0 + 2 * i + (1 + d), (1 + d) % 2, (f[0] + 2 * i, f[1]), False, False)
                    for j in (STEPS - 2, STEPS - 1):
                        step(j0 + j, j % 2, plus(u0, 6 * j - 2), False, False, last=9 * p + e + 1 if j == STEPS - 1 else None)

                expert(0, True)
                with dve.Fori(1, E) as e:
                    expert(e, False)
                gated(E * p + E - 1, E * (p + 1))
                combined(E * p + E - 1)
                dve.wait_ge(s_acc, 4 * E * (p + 1) + 1)

            experts(0)
            flag = dve.value_load(over_i[0:1, 0:1], min_val=0, max_val=1)
            with dve.If(flag > 0):
                experts(1)
            nc.vector.memset(over[:, :], 0.0).then_inc(s_fin0, 1)
            add_to_residual("post_ffn1", acc, 9, tok_c, s_fin)

        @block.tensor
        def _(pe):
            def turn(name, src, bank0=4):
                k = {"mem": 1, "mix0": 0, "mix1": 0, "mem_again": 1}.get(name)
                for b in range(NB):
                    if name in XN:
                        pe.wait_ge(s_xn, NB * XN[name] + b + 1)
                    elif k is None:
                        pe.wait_ge(s_res, NB * RES[{"xa0": "mix0", "ffn0": "xa0", "xa1": "mix1", "ffn1": "xa1"}[name]] + b + 1)
                    for c in range(NC):
                        dst, tokens = turned(bank0, c)[:, b * P:(b + 1) * P], src[:, b, c * P:(c + 1) * P]
                        if k is None:
                            mm = nc.tensor.transpose(dst, tokens, ident[:, :])
                        else:
                            mm = nc.tensor.matmul(dst, tokens, norm_diag[:, k, b, :], start=True, stop=True)
                        if b == NB - 1:
                            mm.then_inc(s_turn, 1)

            def have_chunk(xt, k, per):
                if xt is not None and k % per == 0:
                    pe.wait_ge(s_xtl, NC * xt + (k + per))

            def chan_unit(n, banks, xt=None):
                q, r = unit(n)
                wait_low(pe, (q, r))
                for i, bank in enumerate(banks):
                    for k in range(NC):
                        have_chunk(xt if i == 0 else None, k, 2)
                        o = slice((i * NC + k) * P, (i * NC + k + 1) * P)
                        mm = three(ps[:, bank, 0:S], xth[:, k, :], xtl[:, k, :], w_hi[:, r % SPLIT, o], w_lo[:, r % SPLIT, o],
                                   k == 0, k == NC - 1, True)
                mm.then_inc(s_used, 1)

            def chan_product(n0, s_copied, first, xt, between=None):
                for i in range(4):
                    if i == 2 and between is not None:
                        between()
                    if i >= 2:
                        pe.wait_ge(s_copied, first + 2 * (i - 1))
                    chan_unit(n0 + i, (4 + 2 * i % 4, 5 + 2 * i % 4), XT[xt] if i == 0 else None)

            def tok_product(n0, xt=None):
                for n in range(2):
                    for half in range(2):
                        q, r = unit(n0 + 2 * n + half)
                        wait_low(pe, (q, r))
                        for k in range(4):
                            kk = 4 * half + k
                            o = slice(k * NT, (k + 1) * NT)
                            have_chunk(XT[xt] if xt and n == 0 else None, kk, 2)
                            for b in range(NB):
                                t = slice(b * P, (b + 1) * P)
                                mm = three(y_ps[:, b, n, :], xth[:, kk, t], xtl[:, kk, t], w_hi[:, r % SPLIT, o],
                                           w_lo[:, r % SPLIT, o], kk == 0, kk == NC - 1, False)
                        mm.then_inc(s_used, 1)

            def have_xt(name):
                pe.wait_ge(s_xtl, NC * (XT[name] + 1))

            def attention(layer):
                turn(f"xa{layer}", res)
                chan_product(U[f"q{layer}"], s_qc, NC * layer, f"xa{layer}")
                pe.wait_ge(s_qc, NC * (layer + 1))
                pe.wait_ge(s_kc, NC * (layer + 1))
                for h in range(HEADS):
                    for b in range(NB):
                        for d in range(2):
                            mm = nc.tensor.matmul(ps[:, 4 + h, b * S:(b + 1) * S], chan_a[:, 2 * h + d, b * P:(b + 1) * P],
                                                  buf_k[:, 2 * h + d, :], start=d == 0, stop=d == 1)
                    mm.then_inc(s_sc, 1)
                for h in range(HEADS):
                    pe.wait_ge(s_pn, NC * layer + NB * (h + 1))
                    for m in range(2):
                        for b in range(NB):
                            mm = nc.tensor.transpose(ps[:, 4 + h, m * S + b * P:m * S + (b + 1) * P],
                                                     chan_b[:, h * NB + b, m * P:(m + 1) * P], ident[:, :])
                    mm.then_inc(s_pt, 1)
                pe.wait_ge(s_vc, 4 * (layer + 1))
                for h in range(HEADS):
                    pe.wait_ge((s_pte, s_pto)[h % 2], 2 * layer + h // 2 + 1)
                    for d in range(2):
                        for m in range(2):
                            mm = nc.tensor.matmul(turned(4, 2 * h + d), buf_v[:, m, (2 * h + d) * P:(2 * h + d + 1) * P],
                                                  buf_c[:, (2 * h + m) * S:(2 * h + m + 1) * S], start=m == 0, stop=m == 1)
                        mm.then_inc(s_ov, 1)
                tok_product(U[f"o{layer}"], f"o{layer}")

            pe.wait_ge(s_const, 2)
            turn("mem", tok_b)
            chan_product(U["k0"], s_kc, 0, "mem", lambda: turn("mix0", res, 0))
            pe.wait_ge(s_f0, NC)
            tok_product(U["v0"])
            have_xt("pooled")
            pe.wait_ge(s_vc, 4)
            q, r = unit(U["pool"])
            wait_low(pe, (q, r))
            for b in range(NB):
                for g in range(len(WINDOWS)):
                    for k in range(2):
                        c, o = 2 * g + k, slice((2 * g + k) * S, (2 * g + k + 1) * S)
                        t = slice(b * P, (b + 1) * P)
                        mm = three(y_tok[:, b, g * S:(g + 1) * S], xth[:, c, t], xtl[:, c, t], w_hi[:, r % SPLIT, o],
                                   w_lo[:, r % SPLIT, o], k == 0, k == 1, False)
            mm.then_inc(s_used, 1)
            attention(0)

            def clear_y(banks, stop=False):
                for bank in banks:
                    mm = nc.tensor.matmul(ps[:, bank, :], zeros[:, :], zeros[:, None, :].broadcast_to([P, 4, P]),
                                          start=True, stop=stop)
                return mm

            def down(half, par, u, dense, stop=False):
                r = u[1]
                wait_low(pe, u)
                for k in range(2):
                    kk = 2 * half + k
                    for b in range(NB if dense else 1):
                        if dense:
                            o = par * 1024 + kk * S + b * P
                            h_hi, h_lo = hn_hi[:, o:o + P], hn_lo[:, o:o + P]
                        else:
                            o = 1024 + par * NT + kk * P
                            h_hi, h_lo = xt_hi[:, o:o + P], xt_lo[:, o:o + P]
                        for n in range(2):
                            o = slice(k * D + n * NT, k * D + (n + 1) * NT)
                            mm = three(ps[:, 2 * b + n, :], h_hi, h_lo, w_hi[:, r % SPLIT, o], w_lo[:, r % SPLIT, o],
                                       False, stop and k == 1, False)
                mm.then_inc(s_used, 1)

            def hidden(bank, u, dense, xt=None):
                for half in range(2):
                    v = plus(u, half)
                    r = v[1]
                    wait_low(pe, v)
                    for k in range(4):
                        kk, o = 4 * half + k, slice(k * NT, (k + 1) * NT)
                        have_chunk(xt, kk, 2 if dense else 4)
                        for b in range(NB if dense else 1):
                            a = kk * S + b * P if dense else kk * P
                            mm = three(ps[:, bank + b, :], xt_hi[:, a:a + P], xt_lo[:, a:a + P], w_hi[:, r % SPLIT, o],
                                       w_lo[:, r % SPLIT, o], kk == 0, kk == NC - 1, False)
                    mm.then_inc(s_used, 1)

            def turn_hidden(j, dense):
                sm, sh, st = (s_mul, s_htl, s_ht) if dense else (m_mul, m_htl, m_ht)
                wait_step(pe, sm, j + 1)
                wait_step(pe, sh, j)
                for c in range(4):
                    for b in range(NB if dense else 1):
                        o = turned(4, c)[:, b * P:(b + 1) * P] if dense else ps[:, 4, c * P:(c + 1) * P]
                        mm = nc.tensor.transpose(o, buf_c[:, b * NT + c * P:b * NT + (c + 1) * P], ident[:, :])
                mm.then_inc(st, 1)

            def step(j, par, u0, first, dense, xt=None, last=None):
                ss, sm, sh = (s_silu, s_mul, s_htl) if dense else (m_silu, m_mul, m_htl)
                wait_step(pe, sh if dense else ss, j)
                hidden(4 if dense else 2, u0, dense, xt)
                wait_step(pe, sm, j)
                hidden(6 if dense else 3, plus(u0, 2), dense)
                if first:
                    return
                if last is not None:
                    gather(last)
                wait_step(pe, sh, j)
                down(0, 1 - par, plus(u0, 4), dense)
                turn_hidden(j, dense)
                down(1, 1 - par, plus(u0, 5), dense)

            turn("ffn0", res, 0)
            u0 = unit(U["ffn"])
            step(0, 0, u0, True, True, XT["ffn0"])
            pe.wait_ge(s_init, 1)
            clear_y(range(4))
            turn_hidden(0, True)
            with pe.Fori(0, STEPS // 2) as i:
                for d in range(2):
                    f = plus(u0, 4 + 6 * d)
                    step(2 * i + (1 + d), (1 + d) % 2, (f[0] + 2 * i, f[1]), False, True)
            pe.wait_ge(s_htl, STEPS)
            down(0, 0, plus(u0, PER_FFN - 2), True)
            down(1, 0, plus(u0, PER_FFN - 1), True, True)

            turn("mix1", res)
            for c in range(NC):
                if c >= 2:
                    pe.wait_ge(s_u, c - 1)
                chan_unit(U["pw1"] + c, (4 + 2 * (c % 2), 5 + 2 * (c % 2)), XT["mix1"] if c == 0 else None)
            pe.wait_ge(s_mem2, 16)
            turn("mem_again", tok_c, 0)
            pe.wait_ge(s_u, NC)
            chan_product(U["k1"], s_kc, NC, "mem_again")
            tok_product(U["v1"])
            pe.wait_ge(s_kc, 2 * NC)
            for i in range(TAPS * len(PE_CHUNKS)):
                n, j = i // TAPS, i % TAPS
                pe.wait_ge(s_diag, i + 1)
                mm = nc.tensor.matmul(ps[:, 6 + n, 0:S], diags[:, i % DIAGS, :], conv_u[:, PE_CHUNKS[n], j:j + S], start=j == 0,
                                      stop=j == TAPS - 1)
                mm.then_inc(s_dused, 1)
            for c in range(NC):
                if c in PE_CHUNKS:
                    pe.wait_ge(s_cb, PE_CHUNKS.index(c) + 1)
                else:
                    g = [c in group for group in GROUPS].index(True)
                    pe.wait_ge(s_cv, TAPS * sum(len(group) for group in GROUPS[:g + 1]))
                mm = nc.tensor.matmul(ps[:, 4, 0:S], ones[:, :], chan_b[:, c, :], start=c == 0, stop=c == NC - 1)
            mm.then_inc(s_ln, 1)
            for c in range(NC):
                pe.wait_ge(s_vq, c + 1)
                mm = nc.tensor.matmul(ps[:, 5, 0:S], ones[:, :], chan_c[:, c, :], start=c == 0, stop=c == NC - 1)
            mm.then_inc(s_ln, 1)
            pe.wait_ge(s_vc, 8)
            tok_product(U["pw2"], "z")
            attention(1)

            turn("ffn1", res)
            pe.wait_ge(s_rl, 1)
            for c in range(NC):
                have_chunk(XT["ffn1"], c, 2)
                o = slice(c * E, (c + 1) * E)
                mm = three(ps[0:E, 2, 0:S], xth[:, c, :], xtl[:, c, :], router_hi[:, o], router_lo[:, o], c == 0, c == NC - 1, True)
            mm.then_inc(s_lg, 1)
            pe.wait_ge(s_lt, 1)
            for b in range(NB):
                mm = nc.tensor.transpose(ps[:, 1, b * E:(b + 1) * E], ln_row[0:E, 0, b * P:(b + 1) * P], ident[0:E, 0:E])
            mm.then_inc(s_lg, 1)
            pe.wait_ge(s_const, 3)
            pe.wait_ge(s_sel, 1)
            chosen = [route[:, 7, b, :] for b in range(NB)]
            nc.tensor.matmul(ps[:, 0, 64:64 + E], upper[:, :], chosen[0], start=True, stop=True)
            nc.tensor.matmul(ps[:, 0, 64 + E:64 + 2 * E], upper[:, :], chosen[1], start=True, stop=False)
            nc.tensor.matmul(ps[:, 0, 64 + E:64 + 2 * E], ones[:, :], chosen[0], start=False, stop=True)
            nc.tensor.matmul(ps[:, 0, 128:128 + E], ones[:, :], chosen[0], start=True, stop=False)
            nc.tensor.matmul(ps[:, 0, 128:128 + E], ones[:, :], chosen[1], start=False, stop=True).then_inc(s_pos, 1)

            def gather(idx):
                pe.wait_ge(s_g, NB * (idx + 1))
                for c in range(NC):
                    for i, (b, part) in enumerate(((0, hn_hi), (0, hn_lo), (1, hn_hi), (1, hn_lo))):
                        mm = nc.tensor.matmul(ps[:, 5 + c // 4, (c % 4) * P:(c % 4 + 1) * P],
                                              part[:, b * D + c * P:b * D + (c + 1) * P], sel[:, b * SLOTS:(b + 1) * SLOTS],
                                              start=i == 0, stop=i == 3)
                    if c % 4 == 3:
                        mm.then_inc(s_gath, 1)

            def combine(idx):
                pe.wait_ge(s_ysl, 2 * (idx + 1))
                pe.wait_ge(s_gt, idx + 1)
                for i, bank in enumerate(COMBINE_BANKS):
                    b, n = i // 2, i % 2
                    for part in (ys_hi, ys_lo):
                        mm = nc.tensor.matmul(ps[:, bank, :], sel_t[:, b * P:(b + 1) * P], part[:, n * NT:(n + 1) * NT],
                                              start=part is ys_hi, stop=part is ys_lo)
                    mm.then_inc(s_comb, 1)

            def turn_selection(count, e, first):
                if not first or count:
                    pe.wait_ge(s_gs, count)
                for b in range(NB):
                    nc.tensor.transpose(ps[:, 7, b * P:(b + 1) * P], sel[:, b * SLOTS:(b + 1) * SLOTS].bitcast(F32), ident[:, :])
                for b in range(NB):
                    mm = nc.tensor.matmul(ps[:, 7, NB * P:NB * P + 1], sel[:, b * SLOTS:(b + 1) * SLOTS].bitcast(F32),
                                          gate[:, bass.ds(e, 1), b], start=b == 0, stop=b == 1)
                mm.then_inc(s_gtp, 1)

            def experts(p):
                if p == 0:
                    pe.wait_ge(s_hnl, NB)
                gather(9 * p)

                def expert(e, first):
                    u0 = moe_unit(p, e, 0)
                    j0 = E * STEPS * p + STEPS * e
                    step(j0, 0, u0, True, False, 9 * p + e + XT["gather"])
                    if not first:
                        combine(E * p + e - 1)
                    elif p == 0:
                        pe.wait_ge(s_over, 1)
                    turn_selection(E * p + e, e, first)
                    turn_hidden(j0, False)
                    if not first or p:
                        pe.wait_ge(s_acc, 4 * (E * p + e) + 1)
                    clear_y((0, 1))
                    with pe.Fori(0, STEPS // 2 - 1) as i:
                        for d in range(2):
                            f = plus(u0, 4 + 6 * d)
                            step(j0 + 2 * i + (1 + d), (1 + d) % 2, (f[0] + 2 * i, f[1]), False, False)
                    for j in (STEPS - 2, STEPS - 1):
                        step(j0 + j, j % 2, plus(u0, 6 * j - 2), False, False, last=9 * p + e + 1 if j == STEPS - 1 else None)
                    wait_step(pe, m_htl, j0 + STEPS)
                    down(0, 0, plus(u0, PER_FFN - 2), False)
                    down(1, 0, plus(u0, PER_FFN - 1), False, True)

                expert(0, True)
                with pe.Fori(1, E) as e:
                    expert(e, False)
                combine(E * p + E - 1)

            experts(0)
            flag = pe.value_load(over_i[0:1, 0:1], min_val=0, max_val=1)
            with pe.If(flag > 0):
                experts(1)


def layout(v):
    def stationary(w):
        k, n = w.shape
        return w.reshape(k // P, P, n // P, P).transpose(1, 2, 0, 3).reshape(P, -1, UNIT).transpose(1, 0, 2)

    def moving(w):
        k, n = w.shape
        return w.reshape(k // P, P, n // NT, NT).transpose(1, 2, 0, 3).reshape(P, -1, UNIT).transpose(1, 0, 2)

    def glu(w):
        a = w.reshape(NC, P, 2, NC, P).transpose(1, 3, 2, 0, 4)
        return a.reshape(P, NC, UNIT).transpose(1, 0, 2)

    def swiglu(gu, down):
        g, u, d = moving(gu[:, :F]), moving(gu[:, F:]), down.reshape(2 * STEPS, 2, P, D).transpose(0, 2, 1, 3).reshape(-1, P, UNIT)
        parts = []
        for j in range(STEPS):
            parts += [g[2 * j:2 * j + 2], u[2 * j:2 * j + 2]]
            if j:
                parts.append(d[2 * j - 2:2 * j])
        return parts + [d[2 * STEPS - 2:]]

    wq, wkv, wo = v["xa_wq"], v["xa_wkv"], v["xa_wo"]
    parts = [stationary(wkv[0][:, :D]), moving(wkv[0][:, D:]),
             v["pool_w"][0].reshape(4, 2, P, S).transpose(2, 0, 1, 3).reshape(1, P, UNIT),
             stationary(wq[0]), moving(wo[0])]
    parts += swiglu(v["ffn_w_gu"][0], v["ffn_w_down"][0])
    parts += [glu(v["conv_pw1_w"][0]), stationary(wkv[1][:, :D]), moving(wkv[1][:, D:]), moving(v["conv_pw2_w"][0]),
              stationary(wq[1]), moving(wo[1])]
    for e in range(E):
        parts += swiglu(v["moe_w_gu"][0, e], v["moe_w_down"][0, e])
    stream = np.empty((UNITS, P, UNIT), np.float32)
    at = 0
    for p in parts:
        stream[at:at + len(p)] = p
        at += len(p)

    def chan(a):
        return a.reshape(-1, P).T

    cols = np.concatenate(
        [chan(a) for a in (v["mem_norm_g"], v["mix_pre_g"][0], v["xa_pre_g"][0], v["ffn_pre_g"][0], v["mix_pre_g"][1],
                           v["xa_pre_g"][1], v["ffn_pre_g"][1], v["conv_pw1_b"][0], v["conv_dw_b"][0], v["conv_ln_g"][0],
                           v["conv_ln_b"][0], v["conv_dw_w"][0])]
        + [v["moe_router"][0].reshape(NC, P, E).transpose(1, 0, 2).reshape(P, NC * E)], axis=1)
    recip = np.concatenate([1.0 / np.minimum(np.arange(S) + 1, w) for w in WINDOWS]).astype(np.float32)
    rows = np.stack([recip, v["pool_b"][0].reshape(D), v["pool_scale"][0], v["mix_post_g"][0], v["xa_post_g"][0],
                     v["ffn_post_g"][0], v["conv_pw2_b"][0], v["mix_post_g"][1], v["xa_post_g"][1], v["ffn_post_g"][1]])
    return {"x": v["x"], "mem": v["mem"], "stream": stream, "cols": cols, "rows": rows}


def kernel(**inputs):
    import concourse.bacc as bacc
    from concourse.bass_utils import run_bass_kernel_spmd

    arrays = {n: np.ascontiguousarray(a) for n, a in layout({n: np.asarray(a) for n, a in inputs.items()}).items()}
    nc = bacc.Bacc("TRN2", target_bir_lowering=False, num_devices=1)
    ins = [nc.dram_tensor(n, a.shape, F32, kind="ExternalInput").ap() for n, a in arrays.items()]
    out = nc.dram_tensor("out", (1, S, D), F32, kind="ExternalOutput").ap()
    build(nc, *ins, out)
    return run_bass_kernel_spmd(nc, [arrays], core_ids=[0]).results[0]["out"]
```
